# Optimizing a Trainium2 kernel written in Bass

```python
import jax, jax.numpy as jnp
from jax import lax
import numpy as np

D_MODEL = 1024
BATCH = 1
SEQ = 512
DEPTH = 1

EXPAND = 2
D_MIX = EXPAND * D_MODEL
HEAD_DIM = 64
D_SSM = D_MIX // 2
D_ATT = D_MIX - D_SSM
H_SSM = D_SSM // HEAD_DIM
H_ATT = D_ATT // HEAD_DIM
SSM_GROUPS = 2
SSM_HPG = H_SSM // SSM_GROUPS
D_STATE = 128
CONV_K = 4
CONV_DIM = D_SSM + 2 * SSM_GROUPS * D_STATE
SSD_CHUNK = 128
DT_MIN = 0.001
DT_MAX = 0.1
ATT_BLOCK = 128
N_EXPERT_GROUPS = 4
EXPERTS_PER_GROUP = 8
N_EXPERTS = N_EXPERT_GROUPS * EXPERTS_PER_GROUP
D_EXPERT = D_MODEL // 4
TOP_K_IN_GROUP = 2
EPS = 1e-6
OFF_Z = 0
OFF_XBC = OFF_Z + D_SSM
OFF_DT = OFF_XBC + CONV_DIM
OFF_Q = OFF_DT + H_SSM
OFF_K = OFF_Q + D_ATT
OFF_V = OFF_K + D_ATT
OFF_F = OFF_V + D_ATT
IN_COLS = OFF_F + H_ATT

kernel_name = "hybrid_ssd_fox_hmoe"

def rmsnorm(x, w):
    xf = x.astype(jnp.float32)
    y = xf * lax.rsqrt(jnp.mean(xf * xf, axis=-1, keepdims=True) + EPS)
    return (y * w.astype(jnp.float32)).astype(x.dtype)

def causal_dwconv(u, w, b):
    out = lax.conv_general_dilated(
        u, w[:, None, :].astype(u.dtype), window_strides=(1,), padding=[(CONV_K - 1, 0)],
        dimension_numbers=('NWC', 'WIO', 'NWC'), feature_group_count=u.shape[-1])
    return out + b.astype(u.dtype)

def ssd_chunked(xs, dt, A, Bm, Cm, d_skip):
    b, s = xs.shape[0], xs.shape[1]
    nc, L = s // SSD_CHUNK, SSD_CHUNK
    G, R, P, N = SSM_GROUPS, SSM_HPG, HEAD_DIM, D_STATE
    X = xs.astype(jnp.float32).reshape(b, nc, L, G, R, P)
    dtc = dt.astype(jnp.float32).reshape(b, nc, L, G, R)
    Bc = Bm.astype(jnp.float32).reshape(b, nc, L, G, N)
    Cc = Cm.astype(jnp.float32).reshape(b, nc, L, G, N)
    a = dtc * A.astype(jnp.float32).reshape(G, R)
    cum = jnp.cumsum(a, axis=2)
    Xdt = X * dtc[..., None]
    cum_t = jnp.moveaxis(cum, 2, -1)
    causal = jnp.tril(jnp.ones((L, L), dtype=bool))
    seg = cum_t[..., :, None] - cum_t[..., None, :]
    decay = jnp.exp(jnp.where(causal, seg, -jnp.inf))
    CB = jnp.einsum('bclgn,bcsgn->bcgls', Cc, Bc)
    y_diag = jnp.einsum('bcgls,bcgrls,bcsgrp->bclgrp', CB, decay, Xdt)
    decay_to_end = jnp.exp(cum[:, :, -1:] - cum)
    states = jnp.einsum('bclgn,bclgr,bclgrp->bcgrpn', Bc, decay_to_end, Xdt)
    chunk_decay = jnp.exp(cum[:, :, -1])

    def step(h, inp):
        dec, st = inp
        return dec[..., None, None] * h + st, h

    h0 = jnp.zeros((b, G, R, P, N), jnp.float32)
    _, h_in = lax.scan(step, h0, (jnp.moveaxis(chunk_decay, 1, 0), jnp.moveaxis(states, 1, 0)))
    h_in = jnp.moveaxis(h_in, 0, 1)
    y_off = jnp.einsum('bclgn,bcgrpn,bclgr->bclgrp', Cc, h_in, jnp.exp(cum))
    y = y_diag + y_off + X * d_skip.astype(jnp.float32).reshape(G, R)[:, :, None]
    return y.reshape(b, s, G * R * P).astype(xs.dtype)

def forgetting_attention(q, k, v, log_f):
    b, s, h, d = q.shape
    nb = s // ATT_BLOCK
    scale = 1.0 / np.sqrt(d).astype(np.float32)
    qt = jnp.transpose(q, (0, 2, 1, 3))
    kt = jnp.transpose(k, (0, 2, 1, 3))
    vt = jnp.transpose(v, (0, 2, 1, 3))
    c = jnp.transpose(jnp.cumsum(log_f, axis=1), (0, 2, 1))
    qb = jnp.moveaxis(qt.reshape(b, h, nb, ATT_BLOCK, d), 2, 0)
    cqb = jnp.moveaxis(c.reshape(b, h, nb, ATT_BLOCK), 2, 0)
    k_pos = jnp.arange(s)

    def one_block(args):
        qi, cq, blk = args
        q_pos = blk * ATT_BLOCK + jnp.arange(ATT_BLOCK)
        logits = jnp.einsum('bhqd,bhkd->bhqk', qi, kt).astype(jnp.float32) * scale
        logits = logits + cq[..., :, None] - c[:, :, None, :]
        logits = jnp.where(k_pos[None, :] <= q_pos[:, None], logits, -jnp.inf)
        p = jax.nn.softmax(logits, axis=-1)
        return jnp.einsum('bhqk,bhkd->bhqd', p.astype(vt.dtype), vt)

    out = lax.map(one_block, (qb, cqb, jnp.arange(nb)))
    out = jnp.moveaxis(out, 0, 2).reshape(b, h, s, d)
    return jnp.transpose(out, (0, 2, 1, 3)).reshape(b, s, h * d)

def hierarchical_moe(x, w_rg, b_rg, w_re, b_re, w_gate, w_up, w_down):
    xf = x.astype(jnp.float32)
    grp_logits = xf @ w_rg.astype(jnp.float32) + b_rg.astype(jnp.float32)
    grp_prob = jax.nn.softmax(grp_logits, axis=-1)
    g_star = jnp.argmax(grp_logits, axis=-1)
    p_g = jnp.take_along_axis(grp_prob, g_star[..., None], axis=-1)
    exp_logits = (xf @ w_re.astype(jnp.float32) + b_re.astype(jnp.float32)).reshape(
        x.shape[0], x.shape[1], N_EXPERT_GROUPS, EXPERTS_PER_GROUP)
    sel = jnp.take_along_axis(exp_logits, g_star[..., None, None], axis=2)[..., 0, :]
    top_val, top_idx = lax.top_k(sel, TOP_K_IN_GROUP)
    w2 = jax.nn.softmax(top_val, axis=-1) * p_g
    expert_id = g_star[..., None] * EXPERTS_PER_GROUP + top_idx
    gates = jnp.sum(jax.nn.one_hot(expert_id, N_EXPERTS, dtype=jnp.float32) * w2[..., None],
                    axis=-2).astype(x.dtype)

    def per_seq(args):
        xi, gi = args
        hid = jax.nn.silu(jnp.einsum('sd,edf->sef', xi, w_gate)) * jnp.einsum('sd,edf->sef', xi, w_up)
        return jnp.einsum('sef,se,efd->sd', hid, gi, w_down)

    return lax.map(per_seq, (x, gates))

def setup_inputs(seed: int = 0) -> dict:
    key = jax.random.key(seed)
    ks = jax.random.split(key, 24)
    f32 = jnp.float32
    nrm = lambda k, shp, sc: (jax.random.normal(k, shp, f32) * sc).astype(f32)
    gain = lambda k, shp: 1.0 + 0.05 * jax.random.normal(k, shp, f32)
    dt0 = jnp.exp(jax.random.uniform(ks[5], (DEPTH, H_SSM), f32, np.log(DT_MIN), np.log(DT_MAX)))
    return {
        "x": jax.random.normal(ks[0], (BATCH, SEQ, D_MODEL), f32),
        "norm_mix_w": gain(ks[1], (DEPTH, D_MODEL)),
        "w_in": nrm(ks[2], (DEPTH, D_MODEL, IN_COLS), D_MODEL ** -0.5),
        "conv_w": nrm(ks[3], (DEPTH, CONV_K, CONV_DIM), CONV_K ** -0.5),
        "conv_b": nrm(ks[4], (DEPTH, CONV_DIM), 0.01),
        "dt_bias": dt0 + jnp.log(-jnp.expm1(-dt0)),
        "a_log": jnp.log(jax.random.uniform(ks[6], (DEPTH, H_SSM), f32, 1.0, 16.0)),
        "d_skip": gain(ks[7], (DEPTH, H_SSM)),
        "ssm_norm_w": gain(ks[8], (DEPTH, D_SSM)),
        "q_norm_w": gain(ks[9], (DEPTH, HEAD_DIM)),
        "k_norm_w": gain(ks[10], (DEPTH, HEAD_DIM)),
        "fox_f_bias": 3.0 + 0.5 * jax.random.normal(ks[11], (DEPTH, H_ATT), f32),
        "att_out_norm_w": gain(ks[12], (DEPTH, D_ATT)),
        "w_out": nrm(ks[13], (DEPTH, D_MIX, D_MODEL), D_MIX ** -0.5),
        "norm_ffn_w": gain(ks[14], (DEPTH, D_MODEL)),
        "w_router_group": nrm(ks[15], (DEPTH, D_MODEL, N_EXPERT_GROUPS), D_MODEL ** -0.5),
        "b_router_group": nrm(ks[16], (DEPTH, N_EXPERT_GROUPS), 0.01),
        "w_router_expert": nrm(ks[17], (DEPTH, D_MODEL, N_EXPERTS), D_MODEL ** -0.5),
        "b_router_expert": nrm(ks[18], (DEPTH, N_EXPERTS), 0.01),
        "w_expert_gate": nrm(ks[19], (DEPTH, N_EXPERTS, D_MODEL, D_EXPERT), D_MODEL ** -0.5),
        "w_expert_up": nrm(ks[20], (DEPTH, N_EXPERTS, D_MODEL, D_EXPERT), D_MODEL ** -0.5),
        "w_expert_down": nrm(ks[21], (DEPTH, N_EXPERTS, D_EXPERT, D_MODEL), D_EXPERT ** -0.5),
    }

def reference(x, norm_mix_w, w_in, conv_w, conv_b, dt_bias, a_log, d_skip, ssm_norm_w,
              q_norm_w, k_norm_w, fox_f_bias, att_out_norm_w, w_out, norm_ffn_w,
              w_router_group, b_router_group, w_router_expert, b_router_expert,
              w_expert_gate, w_expert_up, w_expert_down):
    b, s = x.shape[0], x.shape[1]
    for l in range(DEPTH):
        h = rmsnorm(x, norm_mix_w[l])
        proj = h @ w_in[l]
        z = proj[..., OFF_Z:OFF_XBC]
        xbc = jax.nn.silu(causal_dwconv(proj[..., OFF_XBC:OFF_DT], conv_w[l], conv_b[l]))
        xs = xbc[..., :D_SSM]
        Bm = xbc[..., D_SSM:D_SSM + SSM_GROUPS * D_STATE]
        Cm = xbc[..., D_SSM + SSM_GROUPS * D_STATE:]
        dt = jax.nn.softplus(proj[..., OFF_DT:OFF_Q].astype(jnp.float32) + dt_bias[l].astype(jnp.float32))
        A = -jnp.exp(a_log[l].astype(jnp.float32))
        y_ssm = ssd_chunked(xs, dt, A, Bm, Cm, d_skip[l])
        y_ssm = rmsnorm(y_ssm * jax.nn.silu(z), ssm_norm_w[l])

        q = rmsnorm(proj[..., OFF_Q:OFF_K].reshape(b, s, H_ATT, HEAD_DIM), q_norm_w[l])
        k = rmsnorm(proj[..., OFF_K:OFF_V].reshape(b, s, H_ATT, HEAD_DIM), k_norm_w[l])
        v = proj[..., OFF_V:OFF_F].reshape(b, s, H_ATT, HEAD_DIM)
        log_f = jax.nn.log_sigmoid(proj[..., OFF_F:].astype(jnp.float32) + fox_f_bias[l].astype(jnp.float32))
        y_att = rmsnorm(forgetting_attention(q, k, v, log_f), att_out_norm_w[l])

        x = x + jnp.concatenate([y_ssm, y_att], axis=-1) @ w_out[l]
        x = x + hierarchical_moe(rmsnorm(x, norm_ffn_w[l]), w_router_group[l], b_router_group[l],
                                 w_router_expert[l], b_router_expert[l], w_expert_gate[l],
                                 w_expert_up[l], w_expert_down[l])
    return x


_drawn_inputs = setup_inputs


def setup_inputs(seed=0):
    import zlib

    import numpy as np

    out = dict(_drawn_inputs(seed))
    spreads = {}
    factors = {'conv_b': 4.764, 'b_router_group': 7.827, 'b_router_expert': 6.448}
    for name, (base, spread) in spreads.items():
        noise = np.random.default_rng([zlib.crc32(name.encode()), seed]).standard_normal(out[name].shape)
        drawn = base * np.exp(spread * noise) if base else spread * noise
        out[name] = __import__('jax').numpy.asarray(drawn.astype(out[name].dtype))
    for name, factor in factors.items():
        out[name] = (out[name] * factor).astype(out[name].dtype)
    return out
```

```python
from contextlib import ExitStack

import concourse.bass as bass
from concourse import mybir

ALU = mybir.AluOpType
ACT = mybir.ActivationFunctionType
AX = mybir.AxisListType.X
F32 = mybir.dt.float32
F32R = mybir.dt.float32r
BF16 = mybir.dt.bfloat16
I32 = mybir.dt.int32

P = 128
D = 1024
T = 512
TC = T // P
KC = D // P
H = 16
HD = 64
DS = 1024
CONV_K = 4
OFF_Z, OFF_XBC = 0, DS
OFF_DT = OFF_XBC + DS + 512
OFF_Q = OFF_DT + H
OFF_K = OFF_Q + DS
OFF_V = OFF_K + DS
OFF_F = OFF_V + DS
NG, NEG = 4, 8
NE = NG * NEG
DE = 256
EPS = 1e-6
MASKED = -1e30

CAP = 64
NPAIR = NE // 2
ROUNDS = T // CAP
NO_ROW = 4 * T

BLK = 512
RAW = 6
HL = 10

BLOCKS = ([("xbc", 2), ("xbc", 0), ("xbc", 1), ("z", 0), ("z", 1), ("q", 0), ("q", 1), ("k", 0), ("k", 1),
           ("v", 0), ("v", 1), ("so", 0), ("so", 1), ("ao", 0), ("ao", 1)])
NSLOT = len(BLOCKS) * KC
N_XBC, N_Z, N_QK, N_V, N_SO, N_AO, N_END = 0, 12, 20, 36, 44, 52, 60
FEAT = [8, 9, 10, 11, 0, 1, 2, 3, 4, 5, 6, 7]
TRANSPOSED = [n for n in range(12) if FEAT[n] < 10]
T_X, T_QK, T_SY, T_P, T_AY, T_XN, T_END = 8, 18, 34, 42, 106, 114, 122
NU = TC * H

CV_MIX, CV_SSM, CV_ATT, CV_TAP, CV_CB, CV_Q, CV_K, CV_N = 0, 8, 16, 24, 72, 84, 85, 86


def hybrid_layer(nc, x, norm_mix_w, w_in, conv_w, conv_b, dt_bias, a_log, d_skip, ssm_norm_w, q_norm_w, k_norm_w,
                 fox_f_bias, att_out_norm_w, w_out, norm_ffn_w, w_router_group, b_router_group, w_router_expert,
                 b_router_expert, w_expert_gate, w_expert_up, w_expert_down, out):
    x, out, w_in, w_out = x[0], out[0], w_in[0], w_out[0]
    xn_dram = nc.dram_tensor("xn_rows", [T, D], F32).ap()
    slots_dram = nc.dram_tensor("slots", [T * NE, 4], I32).ap()
    slots_by_pos = slots_dram.rearrange("(s e) w -> s (e w)", e=NE)

    with ExitStack() as ctx:
        uid = [0]

        def sb(name, shape, dt=F32, where=ctx):
            return where.enter_context(nc.sbuf_tensor("s_" + name, shape, dt))

        def overlay(name, kbytes, *groups):
            got = {}
            for group in groups:
                with ExitStack() as inner:
                    for n, shape, dt in group:
                        got[n] = sb(n, shape, dt, inner)
            sb(name, [P, kbytes * 256])
            return got

        sems = {}

        def sem(name):
            if name not in sems:
                sems[name] = ctx.enter_context(nc.semaphore(name))
            return sems[name]

        m = {}
        m.update(overlay("region_w", 52,
                         [("raw", [P, RAW, BLK], F32), ("wh", [P, HL, BLK], F32R), ("wl", [P, HL, BLK], F32R)],
                         [("gu1", [P, 2, 2, KC, DE], F32), ("dn1", [P, 2, 2, D], F32)]))
        m.update(overlay("region_qk", 48,
                         [("xin", [P, TC, D], F32), ("hTf", [P, KC, T], F32)],
                         [("qT", [P, KC, T], F32), ("kT", [P, KC, T], F32), ("X", [P, TC, D], F32)],
                         [("ayTh", [P, KC, T], F32R), ("ayTl", [P, KC, T], F32R)],
                         [("gu2", [P, 2, 2, KC, DE], F32), ("dn2", [P, 2, 2, D], F32)]))
        m.update(overlay("region_h", 16, [("hTh", [P, KC, T], F32R)], [("ya", [P, TC, D], F32)], [("xnT", [P, KC, T], F32)],
                         [("xg", [P, 2, D], F32), ("xgT", [P, 2, KC, P], F32)]))
        m.update(overlay("region_s", 51,
                         [("hTl", [P, KC, T], F32R), ("Btm", [P, TC, 256], F32), ("BC", [P, 4, T], F32),
                          ("up", [P, 2, T + 3], F32), ("acc", [P, 2, T], F32), ("xs", [P, 2, T], F32), ("dtfT", [32, T], F32)],
                         [("pad_s", [P, 28 * 256], F32), ("dec", [P, 2, BLK], F32), ("M", [P, 2, BLK], F32), ("Xs", [P, DS], F32),
                          ("Hst", [P, DS], F32), ("y", [P, DS], F32), ("yo", [P, BLK], F32), ("cbs", [P, 256], F32)],
                         [("gu0", [P, 2, 2, KC, DE], F32), ("dn0", [P, 2, 2, D], F32)]))
        m.update(overlay("region_t", 14,
                         [("sq", [P, BLK], F32), ("qn", [P, 2, BLK], F32), ("slot_init", [P, 512], I32),
                          ("wdtf", [P, KC, 32], F32), ("cb3", [P, TC, 96], BF16), ("vecs", [CV_N, P], F32)]
                         + [(n, [P, TC, 32], F32) for n in ("u", "ab", "ew", "w1", "rw", "cor", "res")],
                         [("Pe", [P, 3, T], F32), ("PT", [P, 2, T], F32), ("yTf", [P, 2, T], F32)],
                         [("wffn", [P, D], F32), ("lgT", [NG + NE, T], F32), ("wr", [P, KC, NG + NE], F32), ("lg", [P, TC, NG + NE], F32),
                          ("gsel", [P, TC, NG, NEG], F32),
                          ("cnt", [P, NE], F32)]
                         + [(n, [P, TC, NEG], F32) for n in ("sel", "sel2", "oh", "t8")]
                         + [(n, [P, TC, NE], F32) for n in ("E1", "E2", "occ", "rank", "t32", "occ_tot")],
                         [("sg", [P, DE], F32), ("hid", [P, DE], F32), ("hidT", [P, 2, DE], F32), ("yrow", [P, 2, D], F32),
                          ("slots", [P, NPAIR, 4], I32), ("slot", [P, 4, 4], I32)],
                         ))
        zs = sb("zs", [P, TC, D])
        ident, tri, stri, ones = (sb(n, [P, P]) for n in ("ident", "tri", "stri", "ones"))
        ident_b, mask_ssd, mask_att = (sb(n, [P, P], BF16) for n in ("ident_b", "mask_ssd", "mask_att"))
        hsel = sb("hsel", [96, 32], BF16)
        crow = sb("crow", [96, T], BF16)
        cvec = sb("cvec", [P, CV_N])
        qkw = sb("qkw", [P, 1])
        eps = sb("eps", [P, 1])
        brow = sb("brow", [P, 32])
        alog, dskip = sb("alog", [P, H]), sb("dskip", [P, H])
        rbias = sb("rbias", [P, NG + NE])
        sp, lf, cum, tot = (sb(n, [P, TC, 32]) for n in ("sp", "lf", "cum", "tot"))
        ncum, ecum, dte, etot = (sb(n, [P, TC, H]) for n in ("ncum", "ecum", "dte", "etot"))
        ea = sb("ea", [P, H])
        ssq, rln, rx = (sb(n, [P, 4]) for n in ("ssq", "rln", "rx"))
        yss, yln, rs_s = (sb(n, [P, 4]) for n in ("yss", "yln", "rs_s"))
        ass, aln, rs_a = (sb(n, [P, 4]) for n in ("ass", "aln", "rs_a"))
        fss, fln, rf = (sb(n, [P, 4]) for n in ("fss", "fln", "rf"))
        qss, qr = (sb(n, [P, 16, 8]) for n in ("qss", "qr"))
        nmax, rsum, rinv = (sb(n, [P, NU]) for n in ("nmax", "rsum", "rinv"))
        iota = sb("iota", [P, NE])
        tok = sb("tok", [P, TC])
        lgT, wr = m["lgT"], m["wr"]
        per_token = sb("per_token", [P, 13, TC])
        r4a, r4b, gi, gm, zg, pg, m1, i1, m2, i2, e2, g1, g2 = (per_token[:, i, :] for i in range(13))
        goh, gex = sb("goh", [P, TC, NG]), sb("gex", [P, TC, NG])
        eid = sb("eid", [P, 2, TC])
        dest = sb("dest", [P, 2, TC])
        dest_i = sb("dest_i", [P, 2, TC], I32)
        pay = sb("pay", [P, 2, TC, 4], I32)
        most = sb("most", [P, 1])
        most_i = sb("most_i", [P, 1], I32)
        slots = m["slots"]
        slot = m["slot"]
        spare = sb("spare", [1, 1])

        ps = [ctx.enter_context(nc.psum_tensor(f"bank{i}", [P, 512], F32)) for i in range(8)]

        raw, wh, wl = m["raw"], m["wh"], m["wl"]
        xin, hTf, hTh, hTl = m["xin"], m["hTf"], m["hTh"], m["hTl"]
        qT, kT, X, ya = m["qT"], m["kT"], m["X"], m["ya"]
        Btm, BC, up, acc, xs = m["Btm"], m["BC"], m["up"], m["acc"], m["xs"]
        dec, M, Xs, Hst, y, yo, cbs = (m[n] for n in ("dec", "M", "Xs", "Hst", "y", "yo", "cbs"))
        Pe, PT, yTf = m["Pe"], m["PT"], m["yTf"]
        V = X

        wdtf, cb3, vecs, u, ab, ew, w1, rw, cor, res = (
            m[n] for n in ("wdtf", "cb3", "vecs", "u", "ab", "ew", "w1", "rw", "cor", "res"))
        cnt = m["cnt"]
        lg, gsel, sel, sel2, oh, t8 = (m[n] for n in ("lg", "gsel", "sel", "sel2", "oh", "t8"))
        E1, E2, occ, rank, t32, occ_tot = (m[n] for n in ("E1", "E2", "occ", "rank", "t32", "occ_tot"))

        def heads(ap, n=HD):
            return ap.rearrange("p (h d) -> p h d", d=n)

        def over(ap, *shape):
            return ap.unsqueeze(len(ap.shape)).broadcast_to(list(shape))

        def slot_source(i):
            kind, j = BLOCKS[i // KC]
            k = i % KC
            if kind in ("so", "ao"):
                r = (DS if kind == "ao" else 0) + k * P
                return w_out[r:r + P, j * BLK:(j + 1) * BLK]
            c = {"xbc": OFF_XBC, "z": OFF_Z, "q": OFF_Q, "k": OFF_K, "v": OFF_V}[kind] + j * BLK
            return w_in[k * P:(k + 1) * P, c:c + BLK]

        def pass_read(eng, n):
            if n < N_Z:
                eng.wait_ge(sem("up_copied"), n + 1)
            elif n < N_QK:
                eng.wait_ge(sem("z_silu"), n - N_Z + 1)
            elif n < N_V:
                eng.wait_ge(sem("qk_scaled"), n - N_QK + 1)
            elif n < N_SO:
                eng.wait_ge(sem("v_copied"), n - N_V + 1)
            else:
                eng.wait_ge(sem("residual_added"), n - N_SO + 1)

        def slot_read(eng, i):
            b, k = divmod(i, KC)
            if k < KC - 1:
                eng.wait_ge(sem("slot_used"), b * (KC - 1) + k + 1)
            else:
                eng.wait_ge(sem("pass_done"), 4 * b + 4)

        def low_made(eng, what, i):
            eng.wait_ge(sem(f"{what}_low_{'dve' if i % 2 else 'pool'}"), i // 2 + 1)

        def low_part(eng, what, i, low, full, high):
            eng.wait_ge(sem(what + "_high"), i + 1)
            eng.tensor_tensor(low, full, high.bitcast(F32), ALU.subtract)\
                .then_inc(sem(f"{what}_low_{'dve' if i % 2 else 'pool'}"), 1)

        def weight_low(eng, i):
            low_part(eng, "w", i, wl[:, i % HL, :], raw[:, i % RAW, :], wh[:, i % HL, :])

        def input_low(eng, k):
            low_part(eng, "hT", k, hTl[:, k, :], hTf[:, k, :], hTh[:, k, :])

        def output_low(eng, k, group):
            hi, lo = ((hTh, hTl), (m["ayTh"], m["ayTl"]))[group]
            low_part(eng, "yT", group * KC + k, lo[:, k, :], yTf[:, k % 2, :], hi[:, k, :])

        def slots_after(n):
            b, j = divmod(n, 4)
            first = b * KC + HL
            took = range(first, first + KC - 1) if j == 2 else range(first + KC - 1, first + KC) if j == 3 else ()
            return [i for i in took if i < NSLOT]

        def t_read(eng, i):
            if i < T_X:
                eng.wait_ge(sem("hT_scaled"), i + 1)
            elif i < T_QK:
                eng.wait_ge(sem("x_rows"), i - T_X + 1)
            elif i < T_SY:
                eng.wait_ge(sem("qkT_stored"), i - T_QK + 1)
            elif i < T_P:
                eng.wait_ge(sem("yT_scaled"), i - T_SY + 1)
            elif i < T_AY:
                pt_stored(eng, i - T_P)
            elif i < T_XN:
                eng.wait_ge(sem("yT_scaled"), KC + i - T_AY + 1)
            else:
                eng.wait_ge(sem("xnT_stored"), i - T_XN + 1)

        def pt_stored(eng, v):
            eng.wait_ge(sem("pt_stored_act" if v % 2 == 0 else "pt_stored_dve"), v // 2 + 1)

        def tbank(i):
            return ps[2 + i % 2]

        def load_weight_slot(sp, i):
            if i >= RAW:
                low_made(sp, "w", i - RAW)
            sp.dma_start(raw[:, i % RAW, :], slot_source(i)).then_inc(sem(f"raw_in{i % RAW}"), 16)

        def weight_buffer(p, r4):
            if isinstance(p, int) and p < 3:
                return p, 2
            return (0, p + 1) if r4 % 2 else (1, p)

        def load_gate_up(sp, p, b, wrap=False):
            e = p % NPAIR if wrap else p
            for half in range(2):
                for which, w in ((0, w_expert_gate), (1, w_expert_up)):
                    src = w[0][bass.ds(e + half * NPAIR, 1)].rearrange("e (k p) f -> p (e k) f", p=P)
                    sp.dma_start(m[f"gu{b}"][:, half, which, :, :], src).then_inc(sem(f"gu_in{b}"), 16)

        def load_down(sp, p, b, wrap=False):
            e = p % NPAIR if wrap else p
            for half in range(2):
                src = w_expert_down[0][bass.ds(e + half * NPAIR, 1)].rearrange("e (k p) n -> p (e k) n", p=P)
                sp.dma_start(m[f"dn{b}"][:, half, :, :], src).then_inc(sem(f"dn_in{b}"), 16)

        def load_experts(sp, p, b, free, wrap=False):
            sp.wait_ge(sem("gate_up_done"), free)
            load_gate_up(sp, p, b, wrap)
            sp.wait_ge(sem("down_done"), free)
            load_down(sp, p, b, wrap)

        def experts(eng, expert):
            for r in range(4):
                expert(r, r, first=r < 2)
            with eng.Fori(1, NPAIR // 4) as it:
                for r in range(4):
                    expert(it * 4 + r, r)
            eng.wait_ge(sem("most_known"), 1)
            over_cap = eng.value_load(most_i[0:1, 0:1])
            with eng.If(over_cap > CAP):
                with eng.Fori(NPAIR // 4, ROUNDS * NPAIR // 4) as it:
                    for r in range(4):
                        expert(it * 4 + r, r)

        block = ctx.enter_context(nc.Block())

        @block.sync
        def _(sp):
            for c in range(TC):
                sp.dma_start(xin[:, c, :], x[c * P:(c + 1) * P, :]).then_inc(sem(f"x_in{c}"), 16)
            for k, (c0) in enumerate((OFF_DT, OFF_F)):
                sp.dma_start(wdtf[:, :, k * H:(k + 1) * H],
                             w_in[:, c0:c0 + H].rearrange("(k p) c -> p k c", p=P)).then_inc(sem("wdtf_in"), 16)
            for i in range(N_AO // 4 * KC):
                load_weight_slot(sp, i)
            sp.wait_ge(sem("sy_transposed"), KC)
            sp.wait_ge(sem("y_squared"), TC)
            sp.dma_start(zs[:, :, :], x.rearrange("(c p) d -> p c d", p=P)).then_inc(sem("residual_in"), 16)
            for i in range(N_AO // 4 * KC, NSLOT):
                load_weight_slot(sp, i)
            sp.wait_ge(sem("pass_done"), N_AO)
            load_gate_up(sp, 0, 0)
            load_down(sp, 0, 0)
            sp.wait_ge(sem("pass_done"), N_END)
            for c in range(TC):
                sp.wait_ge(sem("residual_added"), 12 + c + 1)
                sp.dma_start(out[c * P:(c + 1) * P, :], zs[:, c, :]).then_inc(sem("out_stored"), 16)
            load_gate_up(sp, 1, 1)
            load_down(sp, 1, 1)
            load_gate_up(sp, 2, 2)
            sp.wait_ge(sem("xn_transposed"), KC)
            sp.wait_ge(sem("xn_out"), 16 * TC)
            load_down(sp, 2, 2)
            load_experts(sp, 3, 0, 1)
            load_experts(sp, 4, 1, 2)
            with sp.Fori(2, NPAIR // 2 - 1) as it:
                load_experts(sp, it * 2 + 1, 0, it * 2)
                load_experts(sp, it * 2 + 2, 1, it * 2 + 1)
            load_experts(sp, NPAIR - 1, 0, NPAIR - 2)
            sp.wait_ge(sem("most_known"), 1)
            over_cap = sp.value_load(most_i[0:1, 0:1])
            with sp.If(over_cap > CAP):
                with sp.Fori(NPAIR // 2, ROUNDS * NPAIR // 2) as it:
                    load_experts(sp, it * 2, 1, it * 2 - 1, wrap=True)
                    load_experts(sp, it * 2 + 1, 0, it * 2, wrap=True)
                for j in range(2):
                    sp.wait_ge(sem(f"rows_out{j}"), 16 * (ROUNDS * NPAIR // 2))
            sp.wait_ge(sem("out_stored"), 16 * TC)
            for j in range(2):
                sp.wait_ge(sem(f"rows_out{j}"), 16 * (NPAIR // 2))

        @block.gpsimd
        def _(pool):
            count = [0]

            def step():
                count[0] += 1
                return count[0]

            pool.memset(ones[:], 1.0).then_inc(sem("const_ones"), 1)
            pool.memset(ident[:], 0.0).then_inc(sem("pool_seq"), 1)
            pool.wait_ge(sem("pool_seq"), step())
            pool.affine_select(out=ident[:], in_=ident[:], compare_op=ALU.not_equal, fill=1.0, base=0,
                               pattern=[[-1, P]], channel_multiplier=1).then_inc(sem("const_ident"), 1)
            pool.wait_ge(sem("const_ident"), 1)
            pool.wait_ge(sem("const_ones"), 1)
            pool.affine_select(out=tri[:], in_=ones[:], compare_op=ALU.is_ge, fill=0.0, base=0,
                               pattern=[[1, P]], channel_multiplier=-1).then_inc(sem("const_tri"), 1)
            pool.affine_select(out=stri[:], in_=ones[:], compare_op=ALU.is_gt, fill=0.0, base=0,
                               pattern=[[1, P]], channel_multiplier=-1).then_inc(sem("const_tri"), 1)
            pool.tensor_copy(ident_b[:], ident[:]).then_inc(sem("pool_seq"), 1)
            pool.wait_ge(sem("pool_seq"), step())
            pool.memset(mask_ssd[:], 0.0).then_inc(sem("pool_seq"), 1)
            pool.wait_ge(sem("pool_seq"), step())
            pool.memset(mask_att[:], 0.0).then_inc(sem("pool_seq"), 1)
            pool.wait_ge(sem("pool_seq"), step())
            pool.affine_select(out=mask_ssd[:], in_=mask_ssd[:], compare_op=ALU.is_ge, fill=MASKED, base=0,
                               pattern=[[1, P]], channel_multiplier=-1).then_inc(sem("pool_seq"), 1)
            pool.wait_ge(sem("pool_seq"), step())
            pool.affine_select(out=mask_att[:], in_=mask_att[:], compare_op=ALU.is_ge, fill=MASKED, base=0,
                               pattern=[[-1, P]], channel_multiplier=1).then_inc(sem("pool_seq"), 1)
            pool.wait_ge(sem("pool_seq"), step())
            pool.memset(hsel[:], 0.0).then_inc(sem("pool_seq"), 1)
            pool.wait_ge(sem("pool_seq"), step())
            for part in range(3):
                last = pool.affine_select(out=hsel[:], in_=hsel[:], compare_op=ALU.not_equal, fill=1.0, base=-32 * part,
                                          pattern=[[-1, 32]], channel_multiplier=1)
                if part < 2:
                    last.then_inc(sem("pool_seq"), 1)
                    pool.wait_ge(sem("pool_seq"), step())
            last.then_inc(sem("const_masks"), 1)
            pool.iota(iota[:], [[1, NE]], base=0, channel_multiplier=0, allow_small_or_imprecise_dtypes=True)\
                .then_inc(sem("pool_seq"), 1)
            pool.wait_ge(sem("pool_seq"), step())
            pool.iota(tok[:], [[P, TC]], base=0, channel_multiplier=1, allow_small_or_imprecise_dtypes=True)\
                .then_inc(sem("pool_seq"), 1)
            pool.wait_ge(sem("pool_seq"), step())
            init = m["slot_init"]
            pool.memset(init[:], 0).then_inc(sem("pool_seq"), 1)
            pool.wait_ge(sem("pool_seq"), step())
            pool.memset(init[:].rearrange("p (s w) -> p s w", w=4)[:, :, 1], NO_ROW).then_inc(sem("pool_seq"), 1)
            pool.wait_ge(sem("pool_seq"), step())
            pool.dma_start(slots_dram.rearrange("(p s) w -> p (s w)", p=P), init[:]).then_inc(sem("slots_cleared"), 16)

            def lows(first, end):
                for i in range(first, end, 2):
                    weight_low(pool, i)

            for k in range(0, KC, 2):
                input_low(pool, k)

            def scaled_x(c):
                if c < TC - 1:
                    if c:
                        pool.wait_ge(sem("state_done"), 2 * c)
                    pool.tensor_tensor(heads(Xs[:]), heads(X[:, c, :]), over(dte[:, c, :], P, H, HD), ALU.mult)\
                        .then_inc(sem("x_to_end"), 1)
                if c:
                    pool.wait_ge(sem("gated"), c)
                pool.tensor_tensor(heads(y[:]), heads(X[:, c, :]), over(dskip[:], P, H, HD), ALU.mult)\
                    .then_inc(sem("y_skip"), 1)

            def gate(c):
                pool.wait_ge(sem("y_whole"), 2 * c + 2)
                pool.wait_ge(sem("z_silu"), TC + c + 1)
                pool.tensor_tensor(zs[:, c, :], y[:], zs[:, c, :], ALU.mult).then_inc(sem("gated"), 1)

            lows(0, KC * 5)
            pool.wait_ge(sem("scales_known"), 1)
            pool.wait_ge(sem("x_rows"), 10)
            pool.wait_ge(sem("dskip_in"), 16)
            scaled_x(0)
            for c in range(TC):
                lows(KC * (5 + c), KC * (6 + c))
                if c < TC - 1:
                    gate(c)
                    scaled_x(c + 1)
            lows(KC * 9, KC * 10)
            gate(TC - 1)
            lows(KC * 10, KC * 11 + HL)
            for k in range(0, KC, 2):
                output_low(pool, k, 0)
            lows(KC * 11 + HL, KC * 13 + HL)
            for k in range(0, KC, 2):
                output_low(pool, k, 1)
            lows(KC * 13 + HL, NSLOT)

            pool.wait_ge(sem("slots_cleared"), 16)
            pool.wait_ge(sem("payload_ready"), 1)
            for k in range(2):
                for c in range(TC):
                    pool.indirect_dma_start(
                        out=slots_dram[:, :], out_offset=bass.IndirectOffsetOnAxis(ap=dest_i[:, k, c:c + 1], axis=0),
                        in_=pay[:, k, c, :], in_offset=None).then_inc(sem("slots_moved"), 16)
            pool.wait_ge(sem("slots_moved"), 16 * (2 * TC))
            pool.wait_ge(sem("xn_out"), 16 * TC)

            def held(n):
                pool.wait_ge(sem("pool_seq"), n + count[0])
                pool.tensor_tensor(spare[0:1, 0:1], ones[0:1, 0:1], ones[0:1, 0:1], ALU.mult).then_inc(sem("pool_seq"), 1)

            def gather(p, r4, n):
                j = r4 % 2
                if r4 >= 2 or not isinstance(p, int):
                    pool.wait_ge(sem("xg_transposed"), p - 1)
                if not isinstance(p, int):
                    pool.wait_ge(sem(f"rows_out{j}"), (p - j) * 8 - 16)
                    pool.wait_ge(sem("y_scaled_act"), p - 3)
                    pool.wait_ge(sem("y_scaled_dve"), p - 3)
                held(n)
                pool.tensor_copy(slot[:, r4, :], slots[:, bass.ds(p, 1), :].rearrange("p a w -> p (a w)"))\
                    .then_inc(sem("pool_seq"), 1)
                held(n + 2)
                pool.indirect_dma_start(out=m["xg"][:, j, :], out_offset=None, in_=xn_dram[:, :],
                                        in_offset=bass.IndirectOffsetOnAxis(ap=slot[:, r4, 0:1], axis=0))\
                    .then_inc(sem(f"xg_in{j}"), 16)

            def gather_more(p, r4, n, row):
                j, e = r4 % 2, p % NPAIR
                pool.wait_ge(sem("xg_transposed"), p - 1)
                pool.wait_ge(sem(f"rows_out{j}"), (p - j) * 8)
                pool.wait_ge(sem("y_scaled_act"), p - 1)
                pool.wait_ge(sem("y_scaled_dve"), p - 1)
                held(n)
                for half in range(2):
                    pool.dma_start(slot[half * CAP:(half + 1) * CAP, r4, :],
                                   slots_by_pos[bass.ds(row, CAP), bass.ds((e + half * NPAIR) * 4, 4)])\
                        .then_inc(sem(f"slot_in{j}"), 16)
                pool.wait_ge(sem(f"slot_in{j}"), (p - j) * 16 - NPAIR * 16 + 32)
                held(n + 1)
                pool.indirect_dma_start(out=m["xg"][:, j, :], out_offset=None, in_=xn_dram[:, :],
                                        in_offset=bass.IndirectOffsetOnAxis(ap=slot[:, r4, 0:1], axis=0))\
                    .then_inc(sem(f"xg_in{j}"), 16)

            def scatter(p, r4, n):
                j = r4 % 2
                if not isinstance(p, int) or p:
                    pool.wait_ge(sem(f"rows_out{1 - j}"), (p + j) * 8)
                pool.wait_ge(sem("y_scaled_act"), p + 1)
                pool.wait_ge(sem("y_scaled_dve"), p + 1)
                held(n)
                pool.indirect_dma_start(out=out[:, :], out_offset=bass.IndirectOffsetOnAxis(ap=slot[:, r4, 1:2], axis=0),
                                        in_=m["yrow"][:, j, :], in_offset=None, bounds_check=T - 1, oob_is_err=False,
                                        compute_op=ALU.add).then_inc(sem(f"rows_out{j}"), 16)

            pool.wait_ge(sem("router_read"), 1)
            for half in range(2):
                pool.dma_start(slots[half * CAP:(half + 1) * CAP, :, :].rearrange("p e w -> p (e w)"),
                               slots_by_pos[0:CAP, half * NPAIR * 4:(half + 1) * NPAIR * 4]).then_inc(sem("slots_moved"), 16)
            pool.wait_ge(sem("slots_moved"), 16 * (2 * TC + 2))
            gather(0, 0, 0)
            gather(1, 1, 3)
            pool.wait_ge(sem("out_stored"), 16 * TC)
            for p in range(2, 4):
                gather(p, p, 4 * p - 2)
                scatter(p - 2, p - 2, 4 * p + 1)
            with pool.Fori(1, NPAIR // 4) as it:
                for r4 in range(4):
                    gather(it * 4 + r4, r4, it * 16 + (4 * r4 - 2))
                    scatter(it * 4 + (r4 - 2), (r4 + 2) % 4, it * 16 + (4 * r4 + 1))
            for p in range(NPAIR - 2, NPAIR):
                scatter(p, p % 4, 3 * NPAIR + p)
            pool.wait_ge(sem("most_known"), 1)
            over_cap = pool.value_load(most_i[0:1, 0:1])
            with pool.If(over_cap > CAP):
                with pool.Fori(NPAIR // 4, ROUNDS * NPAIR // 4) as it:
                    for r4 in (0, 2):
                        for j in range(2):
                            gather_more(it * 4 + (r4 + j), r4 + j, it * 12 + (NPAIR + 3 * r4 + 2 * j), (it // (NPAIR // 4)) * CAP)
                        for j in range(2):
                            scatter(it * 4 + (r4 + j), r4 + j, it * 12 + (NPAIR + 3 * r4 + 4 + j))
                for j in range(2):
                    pool.wait_ge(sem(f"rows_out{j}"), 16 * (ROUNDS * NPAIR // 2))

        @block.scalar
        def _(act):
            act.dma_start(vecs[CV_MIX:CV_MIX + 8, :], norm_mix_w[0].rearrange("(k p) -> k p", p=P)).then_inc(sem("vec_in"), 16)
            act.dma_start(vecs[CV_SSM:CV_SSM + 8, :], ssm_norm_w[0].rearrange("(k p) -> k p", p=P)).then_inc(sem("vec_in"), 16)
            act.dma_start(vecs[CV_ATT:CV_ATT + 8, :], att_out_norm_w[0].rearrange("(k p) -> k p", p=P)).then_inc(sem("vec_in"), 16)
            act.dma_start(vecs[CV_TAP:CV_TAP + 48, :], conv_w[0].rearrange("j (f p) -> (j f) p", p=P)).then_inc(sem("vec_in"), 16)
            act.dma_start(vecs[CV_CB:CV_CB + 12, :], conv_b[0].rearrange("(f p) -> f p", p=P)).then_inc(sem("vec_in"), 16)
            for r, w in ((CV_Q, q_norm_w), (CV_K, k_norm_w)):
                for half in range(2):
                    act.dma_start(vecs[r:r + 1, half * HD:(half + 1) * HD], w[0:1, :]).then_inc(sem("vec_in"), 16)
            act.dma_start(brow[:, 0:H], dt_bias[0].partition_broadcast(P)).then_inc(sem("brow_in"), 16)
            act.dma_start(brow[:, H:], fox_f_bias[0].partition_broadcast(P)).then_inc(sem("brow_in"), 16)
            act.dma_start(alog[:], a_log[0].partition_broadcast(P)).then_inc(sem("alog_in"), 16)
            act.dma_start(dskip[:], d_skip[0].partition_broadcast(P)).then_inc(sem("dskip_in"), 16)
            act.dma_start(rbias[:, 0:NG], b_router_group[0].partition_broadcast(P)).then_inc(sem("rbias_in"), 16)
            act.dma_start(rbias[:, NG:], b_router_expert[0].partition_broadcast(P)).then_inc(sem("rbias_in"), 16)

            def rstd(total, ln, r, name, scale, width):
                act.activation(ln, total, ACT.Ln, bias=eps[:], scale=1.0 / width).then_inc(sem(name + "_ln"), 1)
                act.wait_ge(sem(name + "_ln"), scale)
                act.activation(r, ln, ACT.Exp, scale=-0.5).then_inc(sem(name + "_rstd"), 1)

            act.preload_act_table_set("natural_log_exp_and_others")
            act.wait_ge(sem("eps_set"), 1)
            for c in range(TC):
                act.wait_ge(sem(f"x_in{c}"), 16)
                if c:
                    act.wait_ge(sem("x_squared"), c)
                act.activation(hTf[:, 0:2, :].rearrange("p k t -> p (k t)"), xin[:, c, :], ACT.Square, accum_out=ssq[:, c:c + 1])\
                    .then_inc(sem("x_squared"), 1)
            act.wait_ge(sem("x_squared"), TC)
            rstd(ssq[:], rln[:], rx[:], "x", 1, D)
            for k in range(KC):
                act.wait_ge(sem("hT_scaled"), k + 1)
                act.activation(hTh[:, k, :], hTf[:, k, :], ACT.Copy).then_inc(sem("hT_high"), 1)

            def high(i):
                act.wait_ge(sem(f"raw_in{i % RAW}"), 16 * (i // RAW + 1))
                if i >= HL:
                    slot_read(act, i - HL)
                act.activation(wh[:, i % HL, :], raw[:, i % RAW, :], ACT.Copy).then_inc(sem("w_high"), 1)

            for i in range(HL):
                high(i)

            act.wait_ge(sem("dt_abs"), 1)
            act.activation(ew[:], ab[:], ACT.Exp, scale=-1.0).then_inc(sem("dt_exp"), 1)
            act.wait_ge(sem("alog_in"), 16)
            act.activation(ea[:], alog[:], ACT.Exp).then_inc(sem("a_exp"), 1)
            act.wait_ge(sem("dt_one_plus"), 1)
            act.activation(ab[:], w1[:], ACT.Ln).then_inc(sem("dt_ln"), 1)
            def highs_after(n):
                for i in slots_after(n):
                    high(i)

            def silu_x(n):
                act.wait_ge(sem("conv_done"), n + 1)
                f = FEAT[n]
                if f < 8:
                    if n >= 6:
                        act.wait_ge(sem("x_transposed"), n - 2 - 1)
                    dst = xs[:, n % 2, :]
                else:
                    dst = BC[:, f - 8, :]
                act.activation(dst, acc[:, n % 2, :], ACT.Silu).then_inc(sem("x_silu"), 1)

            for n in range(N_XBC, N_Z):
                act.wait_ge(sem("pass_done"), n + 1)
                if n >= 2:
                    act.wait_ge(sem("conv_done"), n - 1)
                act.activation(up[:, n % 2, 3:], ps[n % 2][:], ACT.Copy).then_inc(sem("up_copied"), 1)
                if n:
                    silu_x(n - 1)
                highs_after(n)
            silu_x(N_Z - 1)
            act.wait_ge(sem("ends_known"), 1)
            act.activation(ecum[:], cum[:, :, 0:H], ACT.Exp).then_inc(sem("decays_exp"), 1)
            act.activation(dte[:], res[:, :, 0:H], ACT.Exp).then_inc(sem("decays_exp"), 1)
            act.activation(etot[:], tot[:, :, 0:H], ACT.Exp).then_inc(sem("decays_exp"), 1)
            for n in range(N_Z, N_QK):
                i = n - N_Z
                act.wait_ge(sem("pass_done"), n + 1)
                act.activation(zs[:, n % 4, (i // 4) * BLK:(i // 4 + 1) * BLK], ps[n % 2][:], ACT.Silu)\
                    .then_inc(sem("z_silu"), 1)
                highs_after(n)

            def qk_square(i):
                act.wait_ge(sem("pass_done"), N_QK + i + 1)
                if i:
                    act.wait_ge(sem("qk_sum"), i)
                act.activation(m["sq"][:], ps[i % 2][:], ACT.Square).then_inc(sem("qk_squared"), 1)

            def qk_rstd(i):
                act.wait_ge(sem("qk_sum"), i + 1)
                rstd(qss[:, i, :], qss[:, i, :], qr[:, i, :], "qk", i + 1, HD)

            def qk_store(i):
                act.wait_ge(sem("qk_transposed"), i + 1)
                b, c = (i // 4) % 2, i % 4
                dst = (qT if i < 8 else kT)[:, 4 * b:4 * b + 4, c * P:(c + 1) * P]
                src = tbank(T_QK + i)[:].rearrange("p (r t) -> p r t", r=4)
                act.activation(dst, src, ACT.Copy, scale=qkw[:] if i < 8 else 1.0).then_inc(sem("qkT_stored"), 1)

            def decays(c, w):
                act.wait_ge(sem("seg_done"), 4 * c + w + 1)
                if 4 * c + w >= 2:
                    act.wait_ge(sem("m_done"), 4 * c + w - 1)
                for h in range(4 * w, 4 * w + 4):
                    q = (h % 4) * P
                    last = act.activation(dec[:, w % 2, q:q + P], ps[5 + w % 2][:, q:q + P], ACT.Exp, bias=ncum[:, c, h:h + 1])
                last.then_inc(sem("decay_exp"), 1)

            def cb_copy(c):
                act.wait_ge(sem("cb_done"), c + 1)
                if c:
                    act.wait_ge(sem("m_done"), 4 * c)
                act.activation(cbs[:], ps[4][:, 0:256], ACT.Copy).then_inc(sem("cb_copied"), 1)

            def y_square(c):
                act.wait_ge(sem("gated"), c + 1)
                act.activation(Xs[:], zs[:, c, :], ACT.Square, accum_out=yss[:, c:c + 1]).then_inc(sem("y_squared"), 1)
                act.wait_ge(sem("y_squared"), c + 1)

            for i in range(16):
                n = N_QK + i
                qk_square(i)
                qk_rstd(i)
                if i:
                    qk_store(i - 1)
                if i % 4 == 0:
                    cb_copy(i // 4)
                    decays(i // 4, 0)
                    decays(i // 4, 1)
                if i % 4 == 1:
                    decays(i // 4, 2)
                    decays(i // 4, 3)
                highs_after(n)
            qk_store(15)
            for i in range(8):
                n = N_V + i
                act.wait_ge(sem("pass_done"), n + 1)
                if i == 0:
                    act.wait_ge(sem("diag_done"), 4 * TC)
                    act.wait_ge(sem("y_skip"), TC)
                act.activation(V[:, i % 4, (i // 4) * BLK:(i // 4 + 1) * BLK], ps[n % 2][:], ACT.Copy).then_inc(sem("v_copied"), 1)
                highs_after(n)
                if i == 2:
                    for c in range(TC):
                        y_square(c)
                    rstd(yss[:], yln[:], rs_s[:], "y", 1, DS)

            def y_high(k, group):
                act.wait_ge(sem("yT_scaled"), group * KC + k + 1)
                if k == 0:
                    act.wait_ge(sem("pass_done"), N_SO - 1 if group == 0 else N_AO - 1 + 1)
                hi = (hTh, m["ayTh"])[group]
                act.activation(hi[:, k, :], yTf[:, k % 2, :], ACT.Copy).then_inc(sem("yT_high"), 1)

            for k in range(KC):
                y_high(k, 0)
            for n in range(N_SO, N_AO):
                act.wait_ge(sem("pass_done"), n + 1)
                highs_after(n)

            def p_exp(v):
                n = P * (v // H + 1)
                act.wait_ge(sem("max_known"), v + 1)
                if v >= 3:
                    act.wait_ge(sem("p_transposed"), v - 2)
                act.activation(Pe[:, v % 3, 0:n], ps[4 + v % 3][:, 0:n], ACT.Exp, bias=nmax[:, v:v + 1],
                               accum_out=rsum[:, v:v + 1]).then_inc(sem("p_exp"), 1)

            def pt_store(v):
                n = P * (v // H + 1)
                act.wait_ge(sem("p_transposed"), v + 1)
                if v >= 2:
                    act.wait_ge(sem("pv_done"), v - 1)
                act.activation(PT[:, v % 2, 0:n], tbank(T_P + v)[:, 0:n], ACT.Copy).then_inc(sem("pt_stored_act"), 1)

            act.wait_ge(sem("slots_cleared"), 16)
            for v in range(NU + 1):
                if v < NU:
                    p_exp(v)
                if v >= 1 and (v - 1) % 2 == 0:
                    pt_store(v - 1)
            act.preload_act_table_set("natural_log")
            for c in range(TC):
                act.wait_ge(sem("ya_stored"), 2 * c + 2)
                if c:
                    act.wait_ge(sem("ya_squared"), c)
                else:
                    act.wait_ge(sem("p_transposed"), NU)
                act.activation(Pe[:, 0:2, :].rearrange("p a t -> p (a t)"), ya[:, c, :], ACT.Square, accum_out=ass[:, c:c + 1]).then_inc(sem("ya_squared"), 1)
            act.wait_ge(sem("ya_squared"), TC)
            rstd(ass[:], aln[:], rs_a[:], "ya", 1, DS)
            for k in range(KC):
                if k == 0:
                    act.wait_ge(sem("s_done"), NU)
                y_high(k, 1)
            for n in range(N_AO, N_AO + 4):
                act.wait_ge(sem("pass_done"), n + 1)
                highs_after(n)

            act.preload_act_table_set("natural_log")
            act.dma_start(m["wffn"][:], norm_ffn_w[0].partition_broadcast(P)).then_inc(sem("wffn_in"), 16)
            act.dma_start(wr[:, :, 0:NG], w_router_group[0].rearrange("(k p) g -> p k g", p=P)).then_inc(sem("wr_in"), 16)
            act.dma_start(wr[:, :, NG:], w_router_expert[0].rearrange("(k p) g -> p k g", p=P)).then_inc(sem("wr_in"), 16)
            for c in range(TC):
                act.wait_ge(sem("residual_added"), 12 + c + 1)
                if c:
                    act.wait_ge(sem("f_squared"), c)
                act.activation(m["xnT"][:, 0:2, :].rearrange("p k t -> p (k t)"), zs[:, c, :], ACT.Square, accum_out=fss[:, c:c + 1]).then_inc(sem("f_squared"), 1)
            act.wait_ge(sem("f_squared"), TC)
            rstd(fss[:], fln[:], rf[:], "f", 1, D)
            for c in range(TC):
                act.wait_ge(sem("xn_scaled"), c + 1)
                act.dma_start(xn_dram[c * P:(c + 1) * P, :], X[:, c, :]).then_inc(sem("xn_out"), 16)
            for k in range(KC):
                act.wait_ge(sem("xn_transposed"), k + 1)
                act.activation(m["xnT"][:, k, :], tbank(T_XN + k)[:], ACT.Copy).then_inc(sem("xnT_stored"), 1)
            act.wait_ge(sem("group_shifted"), 1)
            act.activation(gex[:], gex[:], ACT.Exp).then_inc(sem("group_exp"), 1)
            act.wait_ge(sem("pair_diff"), 1)
            act.activation(e2, e2, ACT.Exp).then_inc(sem("pair_exp"), 1)

            def expert(p, r4, first=False):
                j = r4 % 2
                act.wait_ge(sem("xg_transposed"), p + 1)
                if not first:
                    act.wait_ge(sem("gate_up_done"), p - 1)
                act.activation(m["xgT"][:, j, 0:4, :].rearrange("p k t -> p (k t)"), ps[2][:], ACT.Copy).then_inc(sem("xgT_act"), 1)
                act.wait_ge(sem("gate_up_done"), p + 1)
                if not first or j:
                    act.wait_ge(sem("hid_done"), p)
                act.activation(m["sg"][:], ps[j][:, 0:DE], ACT.Silu).then_inc(sem("gate_silu"), 1)
                act.wait_ge(sem("down_done"), p + 1)
                if not first:
                    act.wait_ge(sem(f"rows_out{j}"), (p - j) * 8)
                act.activation(m["yrow"][:, j, 0:BLK], ps[6][:], ACT.Copy, scale=slot[:, r4, 2:3].bitcast(F32))\
                    .then_inc(sem("y_scaled_act"), 1)

            experts(act, expert)

        @block.tensor
        def _(pe):
            pe.wait_ge(sem("const_ident"), 1)
            pe.wait_ge(sem("vec_in"), 16 * 9)
            pe.transpose(ps[7][:, 0:CV_N], vecs[:], ident[0:CV_N, 0:CV_N]).then_inc(sem("cvec_done"), 1)
            for k in range(KC):
                if k >= 2:
                    t_read(pe, k - 2)
                for c in range(TC):
                    pe.wait_ge(sem("x_scaled"), c + 1)
                    last = pe.transpose(tbank(k)[:, c * P:(c + 1) * P], xin[:, c, k * P:(k + 1) * P], ident[:])
                last.then_inc(sem("hT_done"), 1)
            pe.wait_ge(sem("wdtf_in"), 16 * 2)
            for k in range(KC):
                pe.wait_ge(sem("hT_scaled"), k + 1)
                last = pe.matmul(ps[5][0:32, :], wdtf[:, k, :], hTf[:, k, :], start=(k == 0), stop=(k == KC - 1))
            last.then_inc(sem("dtf_done"), 1)

            def three(dst, ah, al, bh, bl, start, stop):
                pe.matmul(dst, ah, bh, start=start, stop=False)
                pe.matmul(dst, ah, bl, start=False, stop=False)
                return pe.matmul(dst, al, bh, start=False, stop=stop)

            def one_pass(n):
                b, j = divmod(n, 4)
                kind = BLOCKS[b][0]
                if n >= 2 and n not in (N_AO, N_AO + 1):
                    pass_read(pe, n - 2)
                if n in (N_AO, N_AO + 1):
                    pe.wait_ge(sem("ya_stored"), 6 + n - N_AO + 1)
                hi, lo = (m["ayTh"], m["ayTl"]) if kind == "ao" else (hTh, hTl)
                for k in range(KC):
                    i = b * KC + k
                    if j == 0:
                        low_made(pe, "w", i)
                        if kind == "so":
                            low_made(pe, "yT", k)
                        elif kind == "ao":
                            low_made(pe, "yT", KC + k)
                        elif n == 0:
                            low_made(pe, "hT", k)
                    s = i % HL
                    if kind == "xbc":
                        f = slice(j * P, (j + 1) * P)
                        last = three(ps[n % 2][:], wh[:, s, f], wl[:, s, f], hTh[:, k, :], hTl[:, k, :], k == 0, k == KC - 1)
                    else:
                        t = slice(j * P, (j + 1) * P)
                        last = three(ps[n % 2][:], hi[:, k, t], lo[:, k, t], wh[:, s, :], wl[:, s, :], k == 0, k == KC - 1)
                    if j == 3 and k < KC - 1:
                        last.then_inc(sem("slot_used"), 1)
                last.then_inc(sem("pass_done"), 1)

            def x_transpose(q):
                n = TRANSPOSED[q]
                f = FEAT[n]
                pe.wait_ge(sem("x_silu"), n + 1)
                t_read(pe, T_X + q - 2)
                src = xs[:, n % 2, :] if f < 8 else BC[:, f - 8, :]
                for c in range(TC):
                    last = pe.transpose(tbank(T_X + q)[:, c * P:(c + 1) * P], src[:, c * P:(c + 1) * P], ident[:])
                last.then_inc(sem("x_transposed"), 1)

            def small_sums():
                pe.wait_ge(sem("dtf_copied"), 1)
                for c in range(TC):
                    last = pe.transpose(ps[6][:, c * 32:(c + 1) * 32], m["dtfT"][:, c * P:(c + 1) * P], ident[0:32, 0:32])
                last.then_inc(sem("dtf_rows"), 1)

            def small_cums():
                pe.wait_ge(sem("logs_known"), 1)
                pe.wait_ge(sem("const_tri"), 2)
                pe.wait_ge(sem("const_ones"), 1)
                flat = lf[:].rearrange("p c h -> p (c h)")
                pe.matmul(ps[7][:, 0:P], tri[:], flat, start=True, stop=True)
                pe.matmul(ps[7][:, P:2 * P], ones[:], flat, start=True, stop=True).then_inc(sem("cums_done"), 1)

            def small_rows():
                pe.wait_ge(sem("parts_known"), 1)
                pe.wait_ge(sem("const_masks"), 1)
                for c in range(TC):
                    last = pe.transpose(ps[5][0:96, :].bitcast(BF16)[:, c * P:(c + 1) * P], cb3[:, c, :], ident_b[:])
                last.then_inc(sem("crow_done"), 1)

            small_sums()
            tr = 0
            for n in range(N_QK):
                one_pass(n)
                if n == 1:
                    small_cums()
                if n == 3:
                    small_rows()
                while tr < 10 and TRANSPOSED[tr] <= n - 2:
                    x_transpose(tr)
                    tr += 1

            def seg(c, w):
                v = 4 * c + w
                if v >= 2:
                    pe.wait_ge(sem("decay_exp"), v - 1)
                for h in range(4 * w, 4 * w + 4):
                    dst = ps[5 + w % 2][:, (h % 4) * P:(h % 4 + 1) * P]
                    pe.matmul(dst, hsel[:, h:h + 1].broadcast_to([96, P]), crow[:, c * P:(c + 1) * P], start=True, stop=False)
                    last = pe.matmul(dst, ident_b[:], mask_ssd[:], start=False, stop=True)
                last.then_inc(sem("seg_done"), 1)

            def diag(c, w):
                pe.wait_ge(sem("m_done"), 4 * c + w + 1)
                g = w // 2
                if w % 2 == 0:
                    if g:
                        pe.wait_ge(sem("y_diag"), 2 * c + 1)
                    elif c:
                        pe.wait_ge(sem("state_kept"), 2 * c)
                for h in range(4 * w, 4 * w + 4):
                    at = (h % 8) * HD
                    n = P if h % 8 < 7 else HD
                    last = pe.matmul(ps[7][:, at:at + n], M[:, w % 2, (h % 4) * P:(h % 4 + 1) * P], X[:, c, h * HD:h * HD + n],
                                     start=True, stop=True)
                last.then_inc(sem("diag_done"), 1)

            def cb(c):
                if c:
                    pe.wait_ge(sem("state_kept"), 2 * c - 1)
                for g in range(2):
                    last = pe.matmul(ps[4][:, g * P:(g + 1) * P], BC[:, g, c * P:(c + 1) * P], BC[:, 2 + g, c * P:(c + 1) * P],
                                     start=True, stop=True)
                last.then_inc(sem("cb_done"), 1)

            def y_off(c, g):
                if g == 0:
                    pe.wait_ge(sem("cb_copied"), c + 1)
                else:
                    pe.wait_ge(sem("y_off_scaled"), 2 * (c - 1) + 1)
                pe.wait_ge(sem("state_kept"), 2 * (c - 1) + g + 1)
                pe.matmul(ps[4][:], BC[:, 2 + g, c * P:(c + 1) * P], Hst[:, g * BLK:(g + 1) * BLK], start=True, stop=True)\
                    .then_inc(sem("y_off_done"), 1)

            def state(c, g):
                pe.wait_ge(sem("x_to_end"), c + 1)
                if g == 0:
                    if c:
                        pe.wait_ge(sem("y_off_scaled"), 2 * c)
                    else:
                        pe.wait_ge(sem("cb_copied"), 1)
                else:
                    pe.wait_ge(sem("y_diag"), 2 * c + 2)
                pe.matmul(ps[4 if g == 0 else 7][:], Btm[:, c, g * P:(g + 1) * P], Xs[:, g * BLK:(g + 1) * BLK],
                          start=True, stop=True).then_inc(sem("state_done"), 1)

            def qk_transpose(i):
                pe.wait_ge(sem("qk_scaled"), i + 1)
                t_read(pe, T_QK + i - 2)
                for r in range(4):
                    last = pe.transpose(tbank(T_QK + i)[:, r * P:(r + 1) * P], m["qn"][:, i % 2, r * P:(r + 1) * P], ident[:])
                last.then_inc(sem("qk_transposed"), 1)

            pe.wait_ge(sem("crow_copied"), 1)
            for i in range(17):
                if i < 16:
                    one_pass(N_QK + i)
                else:
                    one_pass(N_V)
                if i >= 1:
                    qk_transpose(i - 1)
                if i == 0:
                    cb(0)
                    seg(0, 0)
                    seg(0, 1)
                    continue
                c, step = (i - 1) // 4, (i - 1) % 4
                if step == 0:
                    diag(c, 0)
                    diag(c, 1)
                    seg(c, 2)
                    seg(c, 3)
                    if c:
                        y_off(c, 0)
                if step == 1:
                    if c:
                        y_off(c, 1)
                    diag(c, 2)
                    diag(c, 3)
                if step == 2 and c < TC - 1:
                    state(c, 0)
                    state(c, 1)
                if step == 3 and c < TC - 1:
                    cb(c + 1)
                    seg(c + 1, 0)
                    seg(c + 1, 1)
            for n in range(N_V + 1, N_SO):
                one_pass(n)

            def y_transpose(k, group):
                i = (T_SY, T_AY)[group] + k
                t_read(pe, i - 2)
                src = (zs, ya)[group]
                for c in range(TC):
                    if group == 0:
                        pe.wait_ge(sem("gated"), c + 1)
                    last = pe.transpose(tbank(i)[:, c * P:(c + 1) * P], src[:, c, k * P:(k + 1) * P], ident[:])
                last.then_inc(sem("sy_transposed" if group == 0 else "ay_transposed"), 1)

            for k in range(KC):
                y_transpose(k, 0)
            for n in range(N_SO, N_AO):
                one_pass(n)

            def scores(v):
                qb, h = divmod(v, H)
                n = P * (qb + 1)
                if v >= 3:
                    pe.wait_ge(sem("p_exp"), v - 2)
                r = slice((h % 2) * HD, (h % 2 + 1) * HD)
                s = ps[4 + v % 3]
                pe.matmul(s[:, 0:n], qT[r, h // 2, qb * P:(qb + 1) * P], kT[r, h // 2, 0:n], start=True, stop=False)
                pe.matmul(s[:, 0:n], hsel[:, H + h:H + h + 1].broadcast_to([96, P]), crow[:, 0:n], start=False, stop=True)
                pe.matmul(s[:, qb * P:n], ident_b[:], mask_att[:], start=False, stop=True, skip_group_check=True)\
                    .then_inc(sem("s_done"), 1)

            def p_transpose(v):
                pe.wait_ge(sem("p_exp"), v + 1)
                t_read(pe, T_P + v - 2)
                for kb in range(v // H + 1):
                    last = pe.transpose(tbank(T_P + v)[:, kb * P:(kb + 1) * P], Pe[:, v % 3, kb * P:(kb + 1) * P], ident[:])
                last.then_inc(sem("p_transposed"), 1)

            def pv(v):
                qb, h = divmod(v, H)
                pt_stored(pe, v)
                w = v // 8
                if v % 8 == 0:
                    if w >= 2:
                        pe.wait_ge(sem("ya_stored"), w - 1)
                    else:
                        pe.wait_ge(sem("residual_added"), 6 + w + 1)
                at = (h % 8) * HD
                n = P if h % 8 < 7 else HD
                for kb in range(qb + 1):
                    last = pe.matmul(ps[w % 2][:, at:at + n], PT[:, v % 2, kb * P:(kb + 1) * P], V[:, kb, h * HD:h * HD + n],
                                     start=(kb == 0), stop=(kb == qb))
                last.then_inc(sem("pv_done"), 1)

            pe.wait_ge(sem("v_copied"), 8)
            pe.wait_ge(sem("qkT_stored"), 16)
            for v in range(NU + 3):
                if v < NU:
                    scores(v)
                if 1 <= v <= NU:
                    p_transpose(v - 1)
                if v >= 3:
                    pv(v - 3)
            pe.wait_ge(sem("ya_stored"), 8)
            for k in range(KC):
                y_transpose(k, 1)
            for n in range(N_AO, N_END):
                one_pass(n)

            for k in range(KC):
                t_read(pe, T_XN + k - 2)
                for c in range(TC):
                    pe.wait_ge(sem("xn_scaled"), c + 1)
                    last = pe.transpose(tbank(T_XN + k)[:, c * P:(c + 1) * P], X[:, c, k * P:(k + 1) * P], ident[:])
                last.then_inc(sem("xn_transposed"), 1)
            pe.wait_ge(sem("wr_in"), 16 * 2)
            for k in range(KC):
                pe.wait_ge(sem("xnT_stored"), k + 1)
                last = pe.matmul(ps[4][0:NG + NE, :], wr[:, k, :], m["xnT"][:, k, :], start=(k == 0), stop=(k == KC - 1))
            last.then_inc(sem("router_done"), 1)
            pe.wait_ge(sem("logits_copied"), 1)
            for c in range(TC):
                last = pe.transpose(ps[5][:, c * 36:(c + 1) * 36], lgT[:, c * P:(c + 1) * P], ident[0:36, 0:36])
            last.then_inc(sem("router_rows"), 1)
            pe.wait_ge(sem("occupied"), 1)
            flat = occ[:].rearrange("p c e -> p (c e)")
            pe.matmul(ps[7][:, 0:P], stri[:], flat, start=True, stop=True)
            pe.matmul(ps[7][:, P:2 * P], ones[:], flat, start=True, stop=True).then_inc(sem("ranks_done"), 1)

            def expert(p, r4, first=False):
                j = r4 % 2
                pe.wait_ge(sem(f"xg_in{j}"), (p - j) * 8 + 16)
                if not first or j:
                    pe.wait_ge(sem("xgT_act"), p)
                    pe.wait_ge(sem("xgT_dve"), p)
                for k in range(KC):
                    last = pe.transpose(ps[2 + k // 4][:, (k % 4) * P:(k % 4 + 1) * P], m["xg"][:, j, k * P:(k + 1) * P], ident[:])
                last.then_inc(sem("xg_transposed"), 1)
                b, had = weight_buffer(p, r4)
                pe.wait_ge(sem(f"gu_in{b}"), had * 32)
                pe.wait_ge(sem("xgT_act"), p + 1)
                pe.wait_ge(sem("xgT_dve"), p + 1)
                if not first:
                    pe.wait_ge(sem("hid_done"), p - 1)
                gu, dn = m[f"gu{b}"], m[f"dn{b}"]
                for k in range(KC):
                    for half in range(2):
                        r = slice(half * CAP, (half + 1) * CAP)
                        last = pe.matmul(ps[j][r, :].rearrange("p (w f) -> p w f", w=2), m["xgT"][:, j, k, r],
                                         gu[:, half, :, k, :], start=(k == 0), stop=(k == KC - 1))
                last.then_inc(sem("gate_up_done"), 1)
                pe.wait_ge(sem("hid_done"), p + 1)
                if not first or j:
                    pe.wait_ge(sem("hidT_stored"), p)
                for q in range(2):
                    last = pe.transpose(ps[4][:, q * P:(q + 1) * P], m["hid"][:, q * P:(q + 1) * P], ident[:])
                last.then_inc(sem("hid_transposed"), 1)
                pe.wait_ge(sem("hidT_stored"), p + 1)
                pe.wait_ge(sem(f"dn_in{b}"), had * 16)
                if not first or j:
                    pe.wait_ge(sem("y_scaled_act"), p)
                    pe.wait_ge(sem("y_scaled_dve"), p)
                for nb in range(2):
                    for q in range(2):
                        for half in range(2):
                            r = slice(half * CAP, (half + 1) * CAP)
                            at = q * P + half * CAP
                            last = pe.matmul(ps[6 + nb][r, :], m["hidT"][:, j, at:at + CAP], dn[:, half, q, nb * BLK:(nb + 1) * BLK],
                                             start=(q == 0), stop=(q == 1))
                last.then_inc(sem("down_done"), 1)

            experts(pe, expert)

        @block.vector
        def _(dve):
            count = [0]

            def step():
                count[0] += 1
                return count[0]

            dve.memset(eps[:], EPS).then_inc(sem("eps_set"), 1)
            dve.wait_ge(sem("eps_set"), 1)
            dve.memset(up[:, :, 0:3], 0.0).then_inc(sem("dve_seq"), 1)
            dve.wait_ge(sem("dve_seq"), step())
            dve.wait_ge(sem("cvec_done"), 1)
            dve.tensor_copy(cvec[:], ps[7][:, 0:CV_N]).then_inc(sem("cvec_copied"), 1)
            dve.wait_ge(sem("cvec_copied"), 1)
            dve.scalar_tensor_tensor(out=qkw[:], in0=cvec[:, CV_Q:CV_Q + 1], scalar=HD ** -0.5, in1=cvec[:, CV_K:CV_K + 1],
                                     op0=ALU.mult, op1=ALU.mult).then_inc(sem("qkw_known"), 1)
            dve.wait_ge(sem("qkw_known"), 1)
            dve.wait_ge(sem("x_rstd"), 1)
            for c in range(TC):
                dve.tensor_scalar(xin[:, c, :], xin[:, c, :], rx[:, c:c + 1], None, ALU.mult).then_inc(sem("x_scaled"), 1)
            for k in range(KC):
                dve.wait_ge(sem("hT_done"), k + 1)
                dve.tensor_scalar(hTf[:, k, :], tbank(k)[:], cvec[:, CV_MIX + k:CV_MIX + k + 1], None, ALU.mult)\
                    .then_inc(sem("hT_scaled"), 1)
            dve.wait_ge(sem("dtf_done"), 1)
            dve.tensor_copy(m["dtfT"][:], ps[5][0:32, :]).then_inc(sem("dtf_copied"), 1)
            for k in range(1, KC, 2):
                input_low(dve, k)
            for i in range(1, HL, 2):
                weight_low(dve, i)
            dve.wait_ge(sem("dtf_rows"), 1)
            dve.wait_ge(sem("brow_in"), 16 * 2)
            rows = ps[6][:, 0:P].rearrange("p (c h) -> p c h", c=TC)
            dve.tensor_tensor(u[:], rows, brow[:].unsqueeze(1).broadcast_to([P, TC, 32]), ALU.add)\
                .then_inc(sem("dve_seq"), 1)
            dve.wait_ge(sem("dve_seq"), step())
            dve.tensor_scalar(u[:, :, H:], u[:, :, H:], -1.0, None, ALU.mult).then_inc(sem("dve_seq"), 1)
            dve.wait_ge(sem("dve_seq"), step())
            dve.scalar_tensor_tensor(out=ab[:], in0=u[:], scalar=-1.0, in1=u[:], op0=ALU.mult, op1=ALU.max)\
                .then_inc(sem("dt_abs"), 1)
            dve.wait_ge(sem("dt_abs"), 1)
            dve.wait_ge(sem("dt_exp"), 1)
            dve.tensor_scalar(w1[:], ew[:], 1.0, None, ALU.add).then_inc(sem("dt_one_plus"), 1)
            dve.wait_ge(sem("dt_one_plus"), 1)
            dve.reciprocal(rw[:], w1[:]).then_inc(sem("dve_seq"), 1)
            dve.wait_ge(sem("dve_seq"), step())
            dve.scalar_tensor_tensor(out=cor[:], in0=w1[:], scalar=-1.0, in1=ew[:], op0=ALU.add, op1=ALU.subtract)\
                .then_inc(sem("dve_seq"), 1)
            dve.wait_ge(sem("dve_seq"), step())
            dve.tensor_tensor(cor[:], cor[:], rw[:], ALU.mult).then_inc(sem("dve_seq"), 1)
            dve.wait_ge(sem("dve_seq"), step())
            dve.wait_ge(sem("dt_ln"), 1)
            dve.tensor_tensor(sp[:], ab[:], cor[:], ALU.subtract).then_inc(sem("dve_seq"), 1)
            dve.wait_ge(sem("dve_seq"), step())
            dve.scalar_tensor_tensor(out=sp[:], in0=u[:], scalar=0.0, in1=sp[:], op0=ALU.max, op1=ALU.add)\
                .then_inc(sem("dve_seq"), 1)
            dve.wait_ge(sem("dve_seq"), step())
            dve.wait_ge(sem("a_exp"), 1)
            dve.scalar_tensor_tensor(out=lf[:, :, 0:H], in0=sp[:, :, 0:H], scalar=-1.0,
                                     in1=ea[:].unsqueeze(1).broadcast_to([P, TC, H]), op0=ALU.mult, op1=ALU.mult)\
                .then_inc(sem("dve_seq"), 1)
            dve.wait_ge(sem("dve_seq"), step())
            dve.tensor_scalar(lf[:, :, H:], sp[:, :, H:], -1.0, None, ALU.mult).then_inc(sem("logs_known"), 1)
            dve.wait_ge(sem("logs_known"), 1)
            dve.wait_ge(sem("cums_done"), 1)
            dve.tensor_copy(cum[:], ps[7][:, 0:P].rearrange("p (c h) -> p c h", c=TC)).then_inc(sem("dve_seq"), 1)
            dve.wait_ge(sem("dve_seq"), step())
            dve.tensor_copy(tot[:], ps[7][:, P:2 * P].rearrange("p (c h) -> p c h", c=TC)).then_inc(sem("dve_seq"), 1)
            dve.wait_ge(sem("dve_seq"), step())
            for c in range(TC - 1):
                dve.tensor_tensor(cum[:, c + 1:, H:], cum[:, c + 1:, H:],
                                  tot[:, c:c + 1, H:].broadcast_to([P, TC - 1 - c, H]), ALU.add).then_inc(sem("dve_seq"), 1)
                dve.wait_ge(sem("dve_seq"), step())
            dve.tensor_scalar(cum[:, :, H:], cum[:, :, H:], -1.0, None, ALU.mult).then_inc(sem("dve_seq"), 1)
            dve.wait_ge(sem("dve_seq"), step())
            dve.tensor_scalar(ncum[:], cum[:, :, 0:H], -1.0, None, ALU.mult).then_inc(sem("dve_seq"), 1)
            dve.wait_ge(sem("dve_seq"), step())
            dve.tensor_tensor(res[:, :, 0:H], tot[:, :, 0:H], cum[:, :, 0:H], ALU.subtract).then_inc(sem("ends_known"), 1)
            dve.wait_ge(sem("ends_known"), 1)
            dve.tensor_copy(cb3[:, :, 0:32], cum[:]).then_inc(sem("dve_seq"), 1)
            dve.wait_ge(sem("dve_seq"), step())
            dve.tensor_tensor(u[:], cum[:], cb3[:, :, 0:32], ALU.subtract).then_inc(sem("dve_seq"), 1)
            dve.wait_ge(sem("dve_seq"), step())
            dve.tensor_copy(cb3[:, :, 32:64], u[:]).then_inc(sem("dve_seq"), 1)
            dve.wait_ge(sem("dve_seq"), step())
            dve.tensor_tensor(u[:], u[:], cb3[:, :, 32:64], ALU.subtract).then_inc(sem("dve_seq"), 1)
            dve.wait_ge(sem("dve_seq"), step())
            dve.tensor_copy(cb3[:, :, 64:96], u[:]).then_inc(sem("parts_known"), 1)
            dve.wait_ge(sem("parts_known"), 1)

            def lows_after(n):
                for i in slots_after(n):
                    if i % 2:
                        weight_low(dve, i)

            def crow_copy():
                dve.wait_ge(sem("crow_done"), 1)
                dve.tensor_copy(crow[:], ps[5][0:96, :].bitcast(BF16)[:, 0:T]).then_inc(sem("crow_copied"), 1)

            def conv(n):
                f = FEAT[n]
                dve.wait_ge(sem("up_copied"), n + 1)
                if n >= 2:
                    dve.wait_ge(sem("x_silu"), n - 1)
                tap = [cvec[:, CV_TAP + 12 * t + f:CV_TAP + 12 * t + f + 1] for t in range(CONV_K)]
                a = acc[:, n % 2, :]
                dve.tensor_scalar(a, up[:, n % 2, 3:3 + T], tap[3], cvec[:, CV_CB + f:CV_CB + f + 1], ALU.mult, ALU.add)\
                    .then_inc(sem("dve_seq"), 1)
                dve.wait_ge(sem("dve_seq"), step())
                for t in (2, 1, 0):
                    ins = dve.scalar_tensor_tensor(out=a, in0=up[:, n % 2, t:t + T], scalar=tap[t], in1=a, op0=ALU.mult, op1=ALU.add)
                    if t:
                        ins.then_inc(sem("dve_seq"), 1)
                        dve.wait_ge(sem("dve_seq"), step())
                ins.then_inc(sem("conv_done"), 1)

            def x_rows(q):
                dve.wait_ge(sem("x_transposed"), q + 1)
                f = FEAT[TRANSPOSED[q]]
                dst = X[:, :, f * P:(f + 1) * P] if f < 8 else Btm[:, :, (f - 8) * P:(f - 7) * P]
                dve.tensor_copy(dst, tbank(T_X + q)[:].rearrange("p (c t) -> p c t", c=TC)).then_inc(sem("x_rows"), 1)

            tr = 0
            for n in range(N_QK):
                if n < N_Z:
                    conv(n)
                if n == 3:
                    crow_copy()
                while tr < 10 and TRANSPOSED[tr] <= n - 2:
                    x_rows(tr)
                    tr += 1
                if n == N_Z + 1:
                    dve.wait_ge(sem("decays_exp"), 3)
                    dve.tensor_tensor(dte[:], dte[:], sp[:, :, 0:H], ALU.mult).then_inc(sem("scales_known"), 1)
                    dve.wait_ge(sem("scales_known"), 1)
                lows_after(n)

            def qk_sum(i):
                dve.wait_ge(sem("qk_squared"), i + 1)
                dve.tensor_reduce(qss[:, i, :], heads(m["sq"][:]), AX, ALU.add).then_inc(sem("qk_sum"), 1)

            def qk_scale(i):
                dve.wait_ge(sem("qk_rstd"), i + 1)
                if i >= 2:
                    dve.wait_ge(sem("qk_transposed"), i - 1)
                dve.tensor_tensor(heads(m["qn"][:, i % 2, :]), heads(ps[i % 2][:]), over(qr[:, i, :], P, 8, HD), ALU.mult)\
                    .then_inc(sem("qk_scaled"), 1)

            def m_product(c, w):
                v = 4 * c + w
                dve.wait_ge(sem("decay_exp"), v + 1)
                dve.wait_ge(sem("cb_copied"), c + 1)
                if v >= 2:
                    dve.wait_ge(sem("diag_done"), v - 1)
                g = w // 2
                for h in range(4 * w, 4 * w + 4):
                    q = slice((h % 4) * P, (h % 4 + 1) * P)
                    last = dve.scalar_tensor_tensor(out=M[:, w % 2, q], in0=dec[:, w % 2, q], scalar=sp[:, c, h:h + 1],
                                                    in1=cbs[:, g * P:(g + 1) * P], op0=ALU.mult, op1=ALU.mult)
                last.then_inc(sem("m_done"), 1)

            def y_add(c, g):
                cols = slice(g * BLK, (g + 1) * BLK)
                dve.wait_ge(sem("diag_done"), 4 * c + 2 * g + 2)
                dve.wait_ge(sem("y_skip"), c + 1)
                dve.tensor_tensor(y[:, cols], y[:, cols], ps[7][:], ALU.add).then_inc(sem("y_diag"), 1)
                dve.wait_ge(sem("y_diag"), 2 * c + g + 1)
                if c:
                    dve.wait_ge(sem("y_off_done"), 2 * (c - 1) + g + 1)
                    dve.tensor_tensor(heads(yo[:]), heads(ps[4][:]), over(ecum[:, c, 8 * g:8 * g + 8], P, 8, HD), ALU.mult)\
                        .then_inc(sem("y_off_scaled"), 1)
                    dve.wait_ge(sem("y_off_scaled"), 2 * (c - 1) + g + 1)
                    dve.tensor_tensor(y[:, cols], y[:, cols], yo[:], ALU.add).then_inc(sem("y_whole"), 1)
                else:
                    dve.tensor_copy(y[:, cols], y[:, cols]).then_inc(sem("y_whole"), 1)

            def state_keep(c, g):
                cols = slice(g * BLK, (g + 1) * BLK)
                if c:
                    dve.wait_ge(sem("y_off_done"), 2 * (c - 1) + g + 1)
                    dve.tensor_tensor(heads(Hst[:, cols]), heads(Hst[:, cols]), over(etot[:, c, 8 * g:8 * g + 8], P, 8, HD), ALU.mult)\
                        .then_inc(sem("dve_seq"), 1)
                    dve.wait_ge(sem("dve_seq"), step())
                dve.wait_ge(sem("state_done"), 2 * c + g + 1)
                bank = ps[4 if g == 0 else 7][:]
                if c:
                    dve.tensor_tensor(Hst[:, cols], Hst[:, cols], bank, ALU.add).then_inc(sem("state_kept"), 1)
                else:
                    dve.tensor_copy(Hst[:, cols], bank).then_inc(sem("state_kept"), 1)
                dve.wait_ge(sem("state_kept"), 2 * c + g + 1)

            for i in range(16):
                qk_sum(i)
                qk_scale(i)
                c = i // 4
                if i % 4 == 0:
                    m_product(c, 0)
                    m_product(c, 1)
                if i % 4 == 1:
                    m_product(c, 2)
                    m_product(c, 3)
                    y_add(c, 0)
                if i % 4 == 2:
                    y_add(c, 1)
                if i % 4 == 3 and c < TC - 1:
                    state_keep(c, 0)
                    state_keep(c, 1)
                lows_after(N_QK + i)
            for n in range(N_V, N_SO):
                lows_after(n)

            def yT_scale(k, group):
                dve.wait_ge(sem("sy_transposed" if group == 0 else "ay_transposed"), k + 1)
                if k >= 2:
                    low_made(dve, "yT", group * KC + k - 2)
                col = (CV_SSM, CV_ATT)[group] + k
                dve.tensor_scalar(yTf[:, k % 2, :], tbank((T_SY, T_AY)[group] + k)[:], cvec[:, col:col + 1], None, ALU.mult)\
                    .then_inc(sem("yT_scaled"), 1)

            def add_residual(i):
                n = N_SO + i
                dve.wait_ge(sem("pass_done"), n + 1)
                r = rs_s if i < 8 else rs_a
                dst = zs[:, i % 4, (i // 4 % 2) * BLK:(i // 4 % 2 + 1) * BLK]
                dve.scalar_tensor_tensor(out=dst, in0=ps[n % 2][:], scalar=r[:, i % 4:i % 4 + 1], in1=dst, op0=ALU.mult, op1=ALU.add)\
                    .then_inc(sem("residual_added"), 1)
                lows_after(n)

            def transposed_output(group):
                for k in range(KC + 1):
                    if k < KC:
                        yT_scale(k, group)
                    if k % 2 == 0 and k:
                        output_low(dve, k - 1, group)

            transposed_output(0)
            dve.wait_ge(sem("residual_in"), 16)
            dve.wait_ge(sem("y_rstd"), 1)
            for i in range(8):
                add_residual(i)

            def row_max(v):
                n = P * (v // H + 1)
                dve.wait_ge(sem("s_done"), v + 1)
                dve.tensor_reduce(nmax[:, v:v + 1], ps[4 + v % 3][:, 0:n], AX, ALU.max, negate=True).then_inc(sem("max_known"), 1)

            def pt_store(v):
                n = P * (v // H + 1)
                dve.wait_ge(sem("p_transposed"), v + 1)
                if v >= 2:
                    dve.wait_ge(sem("pv_done"), v - 1)
                dve.tensor_copy(PT[:, v % 2, 0:n], tbank(T_P + v)[:, 0:n]).then_inc(sem("pt_stored_dve"), 1)

            def ya_store(w):
                qb, g = divmod(w, 2)
                dve.wait_ge(sem("pv_done"), 8 * w + 8)
                dve.reciprocal(rinv[:, 8 * w:8 * w + 8], rsum[:, 8 * w:8 * w + 8]).then_inc(sem("dve_seq"), 1)
                dve.wait_ge(sem("dve_seq"), step())
                if w == 0:
                    dve.wait_ge(sem("pass_done"), N_AO)
                dve.tensor_tensor(heads(ya[:, qb, g * BLK:(g + 1) * BLK]), heads(ps[w % 2][:]), over(rinv[:, 8 * w:8 * w + 8], P, 8, HD),
                                  ALU.mult).then_inc(sem("ya_stored"), 1)

            for v in range(NU + 4):
                if v < NU:
                    row_max(v)
                if 1 <= v <= NU and (v - 1) % 2 == 1:
                    pt_store(v - 1)
                if v >= 4 and (v - 4) % 8 == 7:
                    ya_store((v - 4) // 8)
            transposed_output(1)
            dve.wait_ge(sem("ya_rstd"), 1)
            dve.wait_ge(sem("residual_added"), 8)
            for i in range(8, 16):
                add_residual(i)

            dve.wait_ge(sem("f_rstd"), 1)
            dve.wait_ge(sem("wffn_in"), 16)
            dve.wait_ge(sem("residual_added"), 16)
            for c in range(TC):
                dve.scalar_tensor_tensor(out=X[:, c, :], in0=zs[:, c, :], scalar=rf[:, c:c + 1], in1=m["wffn"][:], op0=ALU.mult,
                                         op1=ALU.mult).then_inc(sem("xn_scaled"), 1)

            dve.wait_ge(sem("router_done"), 1)
            dve.tensor_copy(lgT[:], ps[4][0:NG + NE, :]).then_inc(sem("logits_copied"), 1)
            dve.wait_ge(sem("router_rows"), 1)
            dve.wait_ge(sem("rbias_in"), 16 * 2)
            dve.tensor_tensor(lg[:], ps[5][:, 0:TC * 36].rearrange("p (c e) -> p c e", c=TC),
                              rbias[:].unsqueeze(1).broadcast_to([P, TC, 36]), ALU.add).then_inc(sem("dve_seq"), 1)
            dve.wait_ge(sem("dve_seq"), step())

            def first_max(vals, top, at, tmp, n):
                dve.tensor_reduce(top, vals, AX, ALU.max).then_inc(sem("dve_seq"), 1)
                dve.wait_ge(sem("dve_seq"), step())
                dve.tensor_tensor(tmp, vals, over(top, P, TC, n), ALU.is_lt).then_inc(sem("dve_seq"), 1)
                dve.wait_ge(sem("dve_seq"), step())
                dve.scalar_tensor_tensor(out=tmp, in0=tmp, scalar=float(NE), in1=iota[:, 0:n].unsqueeze(1).broadcast_to([P, TC, n]),
                                         op0=ALU.mult, op1=ALU.add).then_inc(sem("dve_seq"), 1)
                dve.wait_ge(sem("dve_seq"), step())
                dve.tensor_reduce(at, tmp, AX, ALU.min).then_inc(sem("dve_seq"), 1)
                dve.wait_ge(sem("dve_seq"), step())

            def one_hot(dst, at, n):
                dve.tensor_tensor(dst, iota[:, 0:n].unsqueeze(1).broadcast_to([P, TC, n]), over(at, P, TC, n), ALU.is_equal)\
                    .then_inc(sem("dve_seq"), 1)
                dve.wait_ge(sem("dve_seq"), step())

            groups = lg[:, :, 0:NG]
            first_max(groups, gm, gi, goh[:], NG)
            dve.tensor_tensor(gex[:], groups, over(gm, P, TC, NG), ALU.subtract).then_inc(sem("group_shifted"), 1)
            dve.wait_ge(sem("group_shifted"), 1)
            one_hot(goh[:], gi, NG)
            for g in range(NG):
                dve.tensor_tensor(gsel[:, :, g, :], lg[:, :, NG + g * NEG:NG + (g + 1) * NEG],
                                  goh[:, :, g:g + 1].broadcast_to([P, TC, NEG]), ALU.mult).then_inc(sem("dve_seq"), 1)
                dve.wait_ge(sem("dve_seq"), step())
            dve.tensor_tensor(gsel[:, :, 0, :], gsel[:, :, 0, :], gsel[:, :, 1, :], ALU.add).then_inc(sem("dve_seq"), 1)
            dve.wait_ge(sem("dve_seq"), step())
            dve.tensor_tensor(gsel[:, :, 2, :], gsel[:, :, 2, :], gsel[:, :, 3, :], ALU.add).then_inc(sem("dve_seq"), 1)
            dve.wait_ge(sem("dve_seq"), step())
            dve.tensor_tensor(sel[:], gsel[:, :, 0, :], gsel[:, :, 2, :], ALU.add).then_inc(sem("dve_seq"), 1)
            dve.wait_ge(sem("dve_seq"), step())
            first_max(sel[:], m1, i1, t8[:], NEG)
            one_hot(oh[:], i1, NEG)
            dve.scalar_tensor_tensor(out=sel2[:], in0=oh[:], scalar=MASKED, in1=sel[:], op0=ALU.mult, op1=ALU.add)\
                .then_inc(sem("dve_seq"), 1)
            dve.wait_ge(sem("dve_seq"), step())
            first_max(sel2[:], m2, i2, t8[:], NEG)
            dve.tensor_tensor(e2, m2, m1, ALU.subtract).then_inc(sem("pair_diff"), 1)
            dve.wait_ge(sem("pair_diff"), 1)
            for k, at in ((0, i1), (1, i2)):
                dve.scalar_tensor_tensor(out=eid[:, k, :], in0=gi, scalar=float(NEG), in1=at, op0=ALU.mult, op1=ALU.add)\
                    .then_inc(sem("dve_seq"), 1)
                dve.wait_ge(sem("dve_seq"), step())
            one_hot(E1[:], eid[:, 0, :], NE)
            one_hot(E2[:], eid[:, 1, :], NE)
            dve.tensor_tensor(occ[:], E1[:], E2[:], ALU.add).then_inc(sem("occupied"), 1)
            dve.wait_ge(sem("occupied"), 1)
            dve.wait_ge(sem("group_exp"), 1)
            dve.tensor_reduce(zg, gex[:], AX, ALU.add).then_inc(sem("dve_seq"), 1)
            dve.wait_ge(sem("dve_seq"), step())
            dve.reciprocal(pg, zg).then_inc(sem("dve_seq"), 1)
            dve.wait_ge(sem("dve_seq"), step())
            dve.wait_ge(sem("pair_exp"), 1)
            dve.tensor_scalar(g2, e2, 1.0, None, ALU.add).then_inc(sem("dve_seq"), 1)
            dve.wait_ge(sem("dve_seq"), step())
            dve.reciprocal(r4a, g2).then_inc(sem("dve_seq"), 1)
            dve.wait_ge(sem("dve_seq"), step())
            dve.tensor_tensor(g1, r4a, pg, ALU.mult).then_inc(sem("dve_seq"), 1)
            dve.wait_ge(sem("dve_seq"), step())
            dve.tensor_tensor(g2, e2, g1, ALU.mult).then_inc(sem("dve_seq"), 1)
            dve.wait_ge(sem("dve_seq"), step())
            dve.wait_ge(sem("ranks_done"), 1)
            dve.tensor_copy(rank[:], ps[7][:, 0:P].rearrange("p (c e) -> p c e", c=TC)).then_inc(sem("dve_seq"), 1)
            dve.wait_ge(sem("dve_seq"), step())
            dve.tensor_copy(occ_tot[:], ps[7][:, P:2 * P].rearrange("p (c e) -> p c e", c=TC)).then_inc(sem("dve_seq"), 1)
            dve.wait_ge(sem("dve_seq"), step())
            for c in range(TC - 1):
                dve.tensor_tensor(rank[:, c + 1:, :], rank[:, c + 1:, :], occ_tot[:, c:c + 1, :].broadcast_to([P, TC - 1 - c, NE]),
                                  ALU.add).then_inc(sem("dve_seq"), 1)
                dve.wait_ge(sem("dve_seq"), step())
            dve.tensor_tensor(cnt[:], occ_tot[:, 0, :], occ_tot[:, 1, :], ALU.add).then_inc(sem("dve_seq"), 1)
            dve.wait_ge(sem("dve_seq"), step())
            dve.tensor_tensor(cnt[:], cnt[:], occ_tot[:, 2, :], ALU.add).then_inc(sem("dve_seq"), 1)
            dve.wait_ge(sem("dve_seq"), step())
            dve.tensor_tensor(cnt[:], cnt[:], occ_tot[:, 3, :], ALU.add).then_inc(sem("dve_seq"), 1)
            dve.wait_ge(sem("dve_seq"), step())
            dve.tensor_reduce(most[:], cnt[:], AX, ALU.max).then_inc(sem("dve_seq"), 1)
            dve.wait_ge(sem("dve_seq"), step())
            dve.tensor_copy(most_i[:], most[:]).then_inc(sem("most_known"), 1)
            for k, E, g in ((0, E1, g1), (1, E2, g2)):
                dve.tensor_tensor(t32[:], E[:], rank[:], ALU.mult).then_inc(sem("dve_seq"), 1)
                dve.wait_ge(sem("dve_seq"), step())
                dve.tensor_reduce(r4b, t32[:], AX, ALU.add).then_inc(sem("dve_seq"), 1)
                dve.wait_ge(sem("dve_seq"), step())
                dve.scalar_tensor_tensor(out=dest[:, k, :], in0=r4b, scalar=float(NE), in1=eid[:, k, :], op0=ALU.mult, op1=ALU.add)\
                    .then_inc(sem("dve_seq"), 1)
                dve.wait_ge(sem("dve_seq"), step())
                dve.tensor_copy(dest_i[:, k, :], dest[:, k, :]).then_inc(sem("dve_seq"), 1)
                dve.wait_ge(sem("dve_seq"), step())
                dve.tensor_copy(pay[:, k, :, 0], tok[:]).then_inc(sem("dve_seq"), 1)
                dve.wait_ge(sem("dve_seq"), step())
                dve.tensor_copy(pay[:, k, :, 1], tok[:]).then_inc(sem("dve_seq"), 1)
                dve.wait_ge(sem("dve_seq"), step())
                dve.tensor_copy(pay[:, k, :, 2].bitcast(F32), g).then_inc(sem("dve_seq"), 1)
                dve.wait_ge(sem("dve_seq"), step())
                dve.tensor_copy(pay[:, k, :, 3], tok[:]).then_inc(sem("dve_seq"), 1)
                dve.wait_ge(sem("dve_seq"), step())
            dve.tensor_copy(r4a, r4b).then_inc(sem("payload_ready"), 1)
            dve.wait_ge(sem("payload_ready"), 1)
            dve.wait_ge(sem("xnT_stored"), KC)
            dve.tensor_copy(r4a, r4b).then_inc(sem("router_read"), 1)

            def expert(p, r4, first=False):
                j = r4 % 2
                dve.wait_ge(sem("xg_transposed"), p + 1)
                if not first:
                    dve.wait_ge(sem("gate_up_done"), p - 1)
                dve.tensor_copy(m["xgT"][:, j, 4:8, :].rearrange("p k t -> p (k t)"), ps[3][:]).then_inc(sem("xgT_dve"), 1)
                dve.wait_ge(sem("gate_silu"), p + 1)
                if not first or j:
                    dve.wait_ge(sem("hid_transposed"), p)
                dve.tensor_tensor(m["hid"][:], m["sg"][:], ps[j][:, DE:], ALU.mult).then_inc(sem("hid_done"), 1)
                dve.wait_ge(sem("hid_transposed"), p + 1)
                if not first:
                    dve.wait_ge(sem("down_done"), p - 1)
                dve.tensor_copy(m["hidT"][:, j, :], ps[4][:, 0:DE]).then_inc(sem("hidT_stored"), 1)
                dve.wait_ge(sem("down_done"), p + 1)
                if not first:
                    dve.wait_ge(sem(f"rows_out{j}"), (p - j) * 8)
                dve.tensor_scalar(m["yrow"][:, j, BLK:], ps[7][:], slot[:, r4, 2:3].bitcast(F32), None, ALU.mult)\
                    .then_inc(sem("y_scaled_dve"), 1)

            experts(dve, expert)


_INS = ["x", "norm_mix_w", "w_in", "conv_w", "conv_b", "dt_bias", "a_log", "d_skip", "ssm_norm_w", "q_norm_w", "k_norm_w",
        "fox_f_bias", "att_out_norm_w", "w_out", "norm_ffn_w", "w_router_group", "b_router_group", "w_router_expert",
        "b_router_expert", "w_expert_gate", "w_expert_up", "w_expert_down"]


def kernel(**inputs):
    import numpy as _np
    import concourse.bacc as _bacc
    from concourse import mybir as _mybir
    from concourse.bass_utils import run_bass_kernel_spmd as _run

    nc = _bacc.Bacc("TRN2", target_bir_lowering=False, num_devices=1)
    arrays, args = {}, []
    for name in _INS:
        a = _np.ascontiguousarray(inputs[name])
        arrays[f"in_{name}_dram"] = a
        args.append(nc.dram_tensor(f"in_{name}_dram", a.shape, _mybir.dt.from_np(a.dtype), kind="ExternalInput").ap())
    args.append(nc.dram_tensor("out_0_dram", (1, T, D), _mybir.dt.float32, kind="ExternalOutput").ap())
    hybrid_layer(nc, *args)
    r = _run(nc, [arrays], core_ids=[0])
    return r.results[0]["out_0_dram"]
```

```python
from contextlib import ExitStack

import concourse.bass as bass
from concourse import mybir

ALU = mybir.AluOpType
ACT = mybir.ActivationFunctionType
AX = mybir.AxisListType.X
F32 = mybir.dt.float32
F32R = mybir.dt.float32r
BF16 = mybir.dt.bfloat16
I32 = mybir.dt.int32

P = 128
D = 1024
T = 512
TC = T // P
KC = D // P
H = 16
HD = 64
DS = 1024
CONV_K = 4
OFF_Z, OFF_XBC = 0, DS
OFF_DT = OFF_XBC + DS + 512
OFF_Q = OFF_DT + H
OFF_K = OFF_Q + DS
OFF_V = OFF_K + DS
OFF_F = OFF_V + DS
NG, NEG = 4, 8
NE = NG * NEG
DE = 256
EPS = 1e-6
MASKED = -1e30

CAP = 64
NPAIR = NE // 2
ROUNDS = T // CAP
NO_ROW = 4 * T

BLK = 512
RAW = 6
HL = 10

BLOCKS = ([("xbc", 2), ("xbc", 0), ("xbc", 1), ("z", 0), ("z", 1), ("q", 0), ("q", 1), ("k", 0), ("k", 1),
           ("v", 0), ("v", 1), ("so", 0), ("so", 1), ("ao", 0), ("ao", 1)])
NSLOT = len(BLOCKS) * KC
N_XBC, N_Z, N_QK, N_V, N_SO, N_AO, N_END = 0, 12, 20, 36, 44, 52, 60
SSD_OUT = {3: (0, 1, 2), 4: (3, 4, 5), 5: (6, 7)}
FEAT = [8, 9, 10, 11, 0, 1, 2, 3, 4, 5, 6, 7]
TRANSPOSED = [n for n in range(12) if FEAT[n] < 10]
T_X, T_QK, T_SY, T_P, T_AY, T_XN, T_END = 8, 18, 34, 42, 106, 114, 122
NU = TC * H

CV_MIX, CV_SSM, CV_ATT, CV_TAP, CV_CB, CV_Q, CV_K, CV_N = 0, 8, 16, 24, 72, 84, 85, 86


def hybrid_layer(nc, x, norm_mix_w, w_in, conv_w, conv_b, dt_bias, a_log, d_skip, ssm_norm_w, q_norm_w, k_norm_w,
                 fox_f_bias, att_out_norm_w, w_out, norm_ffn_w, w_router_group, b_router_group, w_router_expert,
                 b_router_expert, w_expert_gate, w_expert_up, w_expert_down, out):
    x, out, w_in, w_out = x[0], out[0], w_in[0], w_out[0]
    xn_dram = nc.dram_tensor("xn_rows", [T, D], F32).ap()
    slots_dram = nc.dram_tensor("slots", [T * NE, 4], I32).ap()
    slots_by_pos = slots_dram.rearrange("(s e) w -> s (e w)", e=NE)

    with ExitStack() as ctx:
        uid = [0]

        def sb(name, shape, dt=F32, where=ctx):
            return where.enter_context(nc.sbuf_tensor("s_" + name, shape, dt))

        def overlay(name, kbytes, *groups):
            got = {}
            for group in groups:
                with ExitStack() as inner:
                    for n, shape, dt in group:
                        got[n] = sb(n, shape, dt, inner)
            sb(name, [P, kbytes * 256])
            return got

        sems = {}

        def sem(name):
            if name not in sems:
                sems[name] = ctx.enter_context(nc.semaphore(name))
            return sems[name]

        m = {}
        m.update(overlay("region_w", 52,
                         [("raw", [P, RAW, BLK], F32), ("wh", [P, HL, BLK], F32R), ("wl", [P, HL, BLK], F32R)],
                         [("dn1", [P, 2, 2, D], F32), ("gu1", [P, 2, 2, KC, DE], F32)]))
        m.update(overlay("region_qk", 48,
                         [("xin", [P, TC, D], F32), ("hTf", [P, KC, T], F32)],
                         [("qT", [P, KC, T], F32), ("kT", [P, KC, T], F32), ("X", [P, TC, D], F32)],
                         [("ayTh", [P, KC, T], F32R), ("ayTl", [P, KC, T], F32R)],
                         [("xn", [P, TC, D], F32)],
                         [("gu2", [P, 2, 2, KC, DE], F32), ("dn2", [P, 2, 2, D], F32)]))
        m.update(overlay("region_h", 16, [("hTh", [P, KC, T], F32R)], [("ya", [P, TC, D], F32)], [("xnT", [P, KC, T], F32)],
                         [("xg", [P, 2, D], F32), ("xgT", [P, 2, KC, P], F32)]))
        m.update(overlay("region_s", 51,
                         [("hTl", [P, KC, T], F32R), ("Btm", [P, TC, 256], F32), ("BC", [P, 4, T], F32),
                          ("up", [P, 2, T + 3], F32), ("acc", [P, 2, T], F32), ("xs", [P, 2, T], F32), ("dtfT", [P, T // 2], F32)],
                         [("pad_s", [P, 28 * 256], F32), ("dec", [P, 2, BLK], F32), ("M", [P, 2, BLK], F32), ("Xs", [P, DS], F32),
                          ("Hst", [P, DS], F32), ("y", [P, DS], F32), ("yo", [P, BLK], F32), ("cbs", [P, 256], F32)],
                         [("pad_y", [P, 16 * 256], F32), ("syTh", [P, KC, T], F32R), ("syTl", [P, KC, T], F32R)],
                         [("gu0", [P, 2, 2, KC, DE], F32), ("dn0", [P, 2, 2, D], F32)]))
        m.update(overlay("region_t", 14,
                         [("sq", [P, BLK], F32), ("qn", [P, 2, BLK], F32), ("slot_init", [P, 512], I32),
                          ("wdtf", [P, KC, 32], F32), ("cb3", [P, TC, 96], BF16), ("vecs", [CV_N, P], F32)]
                         + [(n, [P, TC, 32], F32) for n in ("u", "ab", "ew", "w1", "rw", "cor", "res")],
                         [("Pe", [P, 3, T], F32), ("PT", [P, 2, T], F32), ("yTf", [P, 2, T], F32)],
                         [("wffn", [P, D], F32), ("lgT", [P, T // 2], F32), ("wr", [P, KC, NG + NE], F32), ("lg", [P, TC, NG + NE], F32),
                          ("gsel", [P, TC, NG, NEG], F32), ("E12", [P, 2, TC, NE], F32), ("t12", [P, 2, TC, NE], F32)]
                         + [(n, [P, TC, NEG], F32) for n in ("sel", "sel2", "oh", "t8")]
                         + [(n, [P, TC, NE], F32) for n in ("occ",)],
                         [("sg", [P, DE], F32), ("hid", [P, DE], F32), ("hidT", [P, 2, DE], F32), ("yrow", [P, 2, D], F32),
                          ("slots", [P, NPAIR, 4], I32), ("slot", [P, 4, 4], I32)],
                         ))
        m.update(overlay("region_z", 16, [("zs", [P, TC, D], F32)], [("dn3", [P, 2, 2, D], F32)]))
        zs = m["zs"]
        ident, tri, stri, ones = (sb(n, [P, P]) for n in ("ident", "tri", "stri", "ones"))
        ident_b, mask_ssd, mask_att = (sb(n, [P, P], BF16) for n in ("ident_b", "mask_ssd", "mask_att"))
        hsel = sb("hsel", [96, 32], BF16)
        crow = sb("crow", [96, T], BF16)
        cvec = sb("cvec", [P, CV_N])
        qkw = sb("qkw", [P, 1])
        eps = sb("eps", [P, 1])
        brow = sb("brow", [P, 32])
        alog, dskip = sb("alog", [P, H]), sb("dskip", [P, H])
        rbias = sb("rbias", [P, NG + NE])
        sp, lf, cum, tot = (sb(n, [P, TC, 32]) for n in ("sp", "lf", "cum", "tot"))
        ncum, ecum, dte, etot = (sb(n, [P, TC, H]) for n in ("ncum", "ecum", "dte", "etot"))
        ea = sb("ea", [P, H])
        ssq, rln, rx = (sb(n, [P, 4]) for n in ("ssq", "rln", "rx"))
        yss, yln, rs_s = (sb(n, [P, 4]) for n in ("yss", "yln", "rs_s"))
        ass, aln, rs_a = (sb(n, [P, 4]) for n in ("ass", "aln", "rs_a"))
        fss, fln, rf = (sb(n, [P, 4]) for n in ("fss", "fln", "rf"))
        qss, qr = (sb(n, [P, 16, 8]) for n in ("qss", "qr"))
        nmax, rsum, rinv = (sb(n, [P, NU]) for n in ("nmax", "rsum", "rinv"))
        iota = sb("iota", [P, NE])
        tok = sb("tok", [P, TC])
        lgT, wr = m["lgT"], m["wr"]
        per_token = sb("per_token", [P, 11, TC])
        inv, gi, gm, zg, pg, m1, i1, m2, i2, e2, e21 = (per_token[:, i, :] for i in range(11))
        goh, gex = sb("goh", [P, TC, NG]), sb("gex", [P, TC, NG])
        eid = sb("eid", [P, 2, TC])
        place = sb("place", [P, 2, TC])
        dest_i = sb("dest_i", [P, 2, TC], I32)
        pay = sb("pay", [P, 2, TC, 4], I32)
        most = sb("most", [P, 1])
        most_i = sb("most_i", [P, 1], I32)
        slots = m["slots"]
        slot = m["slot"]
        spare = sb("spare", [1, 1])

        ps = [ctx.enter_context(nc.psum_tensor(f"bank{i}", [P, 512], F32)) for i in range(8)]

        raw, wh, wl = m["raw"], m["wh"], m["wl"]
        xin, hTf, hTh, hTl = m["xin"], m["hTf"], m["hTh"], m["hTl"]
        qT, kT, X, ya = m["qT"], m["kT"], m["X"], m["ya"]
        Btm, BC, up, acc, xs = m["Btm"], m["BC"], m["up"], m["acc"], m["xs"]
        dec, M, Xs, Hst, y, yo, cbs = (m[n] for n in ("dec", "M", "Xs", "Hst", "y", "yo", "cbs"))
        Pe, PT, yTf = m["Pe"], m["PT"], m["yTf"]
        V = X

        wdtf, cb3, vecs, u, ab, ew, w1, rw, cor, res = (
            m[n] for n in ("wdtf", "cb3", "vecs", "u", "ab", "ew", "w1", "rw", "cor", "res"))
        lg, gsel, sel, sel2, oh, t8 = (m[n] for n in ("lg", "gsel", "sel", "sel2", "oh", "t8"))
        E12, t12, occ, xn = (m[n] for n in ("E12", "t12", "occ", "xn"))

        def heads(ap, n=HD):
            return ap.rearrange("p (h d) -> p h d", d=n)

        def over(ap, *shape):
            return ap.unsqueeze(len(ap.shape)).broadcast_to(list(shape))

        def slot_source(i):
            kind, j = BLOCKS[i // KC]
            k = i % KC
            if kind in ("so", "ao"):
                r = (DS if kind == "ao" else 0) + k * P
                return w_out[r:r + P, j * BLK:(j + 1) * BLK]
            c = {"xbc": OFF_XBC, "z": OFF_Z, "q": OFF_Q, "k": OFF_K, "v": OFF_V}[kind] + j * BLK
            return w_in[k * P:(k + 1) * P, c:c + BLK]

        def pass_read(eng, n):
            if n < N_Z:
                eng.wait_ge(sem("up_copied"), n + 1)
            elif n < N_QK:
                eng.wait_ge(sem("z_silu"), n - N_Z + 1)
            elif n < N_V:
                eng.wait_ge(sem("qk_scaled"), n - N_QK + 1)
            elif n < N_SO:
                eng.wait_ge(sem("v_copied"), n - N_V + 1)
            else:
                eng.wait_ge(sem("residual_added"), n - N_SO + 1)

        def slot_read(eng, i):
            b, k = divmod(i, KC)
            if k < KC - 1:
                eng.wait_ge(sem("slot_used"), b * (KC - 1) + k + 1)
            else:
                eng.wait_ge(sem("pass_done"), 4 * b + 4)

        def low_made(eng, what, i):
            eng.wait_ge(sem(f"{what}_low_{'dve' if i % 2 else 'pool'}"), i // 2 + 1)

        def low_part(eng, what, i, low, full, high):
            eng.wait_ge(sem(what + "_high"), i + 1)
            eng.tensor_tensor(low, full, high.bitcast(F32), ALU.subtract)\
                .then_inc(sem(f"{what}_low_{'dve' if i % 2 else 'pool'}"), 1)

        def weight_low(eng, i):
            low_part(eng, "w", i, wl[:, i % HL, :], raw[:, i % RAW, :], wh[:, i % HL, :])

        def input_low(eng, k):
            low_part(eng, "hT", k, hTl[:, k, :], hTf[:, k, :], hTh[:, k, :])

        def output_low(eng, k, group):
            hi, lo = ((m["syTh"], m["syTl"]), (m["ayTh"], m["ayTl"]))[group]
            low_part(eng, "yT", group * KC + k, lo[:, k, :], yTf[:, k % 2, :], hi[:, k, :])

        def slots_after(n):
            b, j = divmod(n, 4)
            first = b * KC + HL
            took = range(first, first + KC - 1) if j == 2 else range(first + KC - 1, first + KC) if j == 3 else ()
            return [i for i in took if i < NSLOT]

        def t_read(eng, i):
            if i < T_X:
                eng.wait_ge(sem("hT_scaled"), i + 1)
            elif i < T_QK:
                eng.wait_ge(sem("x_rows"), i - T_X + 1)
            elif i < T_SY:
                eng.wait_ge(sem("qkT_stored"), i - T_QK + 1)
            elif i < T_P:
                eng.wait_ge(sem("yT_scaled"), i - T_SY + 1)
            elif i < T_AY:
                pt_stored(eng, i - T_P)
            elif i < T_XN:
                eng.wait_ge(sem("yT_scaled"), KC + i - T_AY + 1)
            else:
                xnT_stored(eng, i - T_XN)

        def xnT_stored(eng, k):
            eng.wait_ge(sem("xnT_stored_act" if k % 2 == 0 else "xnT_stored_dve"), k // 2 + 1)

        def pt_stored(eng, v):
            eng.wait_ge(sem("pt_stored_act" if v % 2 == 0 else "pt_stored_dve"), v // 2 + 1)

        def tbank(i):
            return ps[2 + i % 2]

        def load_weight_slot(sp, i):
            if i >= RAW:
                low_made(sp, "w", i - RAW)
            sp.dma_start(raw[:, i % RAW, :], slot_source(i)).then_inc(sem(f"raw_in{i % RAW}"), 16)

        def gate_up_buffer(p, r4):
            if isinstance(p, int) and p < 3:
                return p, 2
            return (0, p + 1) if r4 % 2 else (1, p)

        def down_buffer(p, r4):
            if isinstance(p, int) and p < 4:
                return p, 2
            return (0, p - 1) if r4 % 2 else (1, p)

        def load_gate_up(sp, p, b, wrap=False, parts=(0, 1, 2, 3)):
            e = p % NPAIR if wrap else p
            for half in range(2):
                for which, w in ((0, w_expert_gate), (1, w_expert_up)):
                    if 2 * half + which not in parts:
                        continue
                    src = w[0][bass.ds(e + half * NPAIR, 1)].rearrange("e (k p) f -> p (e k) f", p=P)
                    sp.dma_start(m[f"gu{b}"][:, half, which, :, :], src).then_inc(sem(f"gu_in{b}"), 16)

        def load_down(sp, p, b, wrap=False):
            e = p % NPAIR if wrap else p
            for half in range(2):
                src = w_expert_down[0][bass.ds(e + half * NPAIR, 1)].rearrange("e (k p) n -> p (e k) n", p=P)
                sp.dma_start(m[f"dn{b}"][:, half, :, :], src).then_inc(sem(f"dn_in{b}"), 16)

        def load_experts(sp, p, b, free, wrap=False):
            sp.wait_ge(sem("gate_up_done"), free)
            load_gate_up(sp, p, b, wrap)
            sp.wait_ge(sem("down_done"), free)
            load_down(sp, p, b, wrap)

        def experts(eng, expert):
            for r in range(4):
                expert(r, r, first=r < 2)
            with eng.Fori(1, NPAIR // 4) as it:
                for r in range(4):
                    expert(it * 4 + r, r)
            eng.wait_ge(sem("most_known"), 1)
            over_cap = eng.value_load(most_i[0:1, 0:1])
            with eng.If(over_cap > CAP):
                with eng.Fori(NPAIR // 4, ROUNDS * NPAIR // 4) as it:
                    for r in range(4):
                        expert(it * 4 + r, r)

        block = ctx.enter_context(nc.Block())

        @block.sync
        def _(sp):
            for c in range(TC):
                sp.dma_start(xin[:, c, :], x[c * P:(c + 1) * P, :]).then_inc(sem(f"x_in{c}"), 16)
            sp.dma_start(vecs[CV_MIX:CV_MIX + 8, :], norm_mix_w[0].rearrange("(k p) -> k p", p=P)).then_inc(sem("vec_in"), 16)
            sp.dma_start(vecs[CV_SSM:CV_SSM + 8, :], ssm_norm_w[0].rearrange("(k p) -> k p", p=P)).then_inc(sem("vec_in"), 16)
            sp.dma_start(vecs[CV_ATT:CV_ATT + 8, :], att_out_norm_w[0].rearrange("(k p) -> k p", p=P)).then_inc(sem("vec_in"), 16)
            sp.dma_start(vecs[CV_TAP:CV_TAP + 48, :], conv_w[0].rearrange("j (f p) -> (j f) p", p=P)).then_inc(sem("vec_in"), 16)
            sp.dma_start(vecs[CV_CB:CV_CB + 12, :], conv_b[0].rearrange("(f p) -> f p", p=P)).then_inc(sem("vec_in"), 16)
            for r, w in ((CV_Q, q_norm_w), (CV_K, k_norm_w)):
                for half in range(2):
                    sp.dma_start(vecs[r:r + 1, half * HD:(half + 1) * HD], w[0:1, :]).then_inc(sem("vec_in"), 16)
            for k, (c0) in enumerate((OFF_DT, OFF_F)):
                sp.dma_start(wdtf[:, :, k * H:(k + 1) * H],
                             w_in[:, c0:c0 + H].rearrange("(k p) c -> p k c", p=P)).then_inc(sem("wdtf_in"), 16)
            for i in range((N_SO // 4 + 1) * KC):
                load_weight_slot(sp, i)
            sp.wait_ge(sem("sy_transposed"), KC)
            sp.wait_ge(sem("y_squared"), TC)
            sp.dma_start(zs[:, :, :], x.rearrange("(c p) d -> p c d", p=P)).then_inc(sem("residual_in"), 16)
            for i in range((N_SO // 4 + 1) * KC, NSLOT):
                load_weight_slot(sp, i)
            sp.wait_ge(sem("pass_done"), N_AO)
            load_gate_up(sp, 0, 0)
            load_down(sp, 0, 0)
            sp.wait_ge(sem("pv_done"), NU)
            load_down(sp, 2, 2)
            sp.wait_ge(sem("pass_done"), N_AO + 4)
            for i in range(NSLOT - RAW, NSLOT):
                low_made(sp, "w", i)
            load_down(sp, 1, 1)
            sp.wait_ge(sem("pass_done"), N_END)
            load_gate_up(sp, 1, 1)
            for c in range(TC):
                sp.wait_ge(sem("residual_added"), 12 + c + 1)
                sp.dma_start(out[c * P:(c + 1) * P, :], zs[:, c, :]).then_inc(sem("out_stored"), 16)
            sp.wait_ge(sem("xn_transposed"), KC)
            sp.wait_ge(sem("xn_out"), 16 * TC)
            load_gate_up(sp, 2, 2, parts=(0, 1, 2))
            sp.wait_ge(sem("xg_in0"), 16)
            load_gate_up(sp, 2, 2, parts=(3,))
            sp.wait_ge(sem("out_stored"), 16 * TC)
            sp.wait_ge(sem("xn_scaled"), TC)
            load_down(sp, 3, 3)
            sp.wait_ge(sem("gate_up_done"), 1)
            load_gate_up(sp, 3, 0)
            sp.wait_ge(sem("down_done"), 1)
            load_down(sp, 5, 0)
            load_experts(sp, 4, 1, 2)
            sp.wait_ge(sem("gate_up_done"), 4)
            load_gate_up(sp, 5, 0)
            with sp.Fori(3, NPAIR // 2) as it:
                load_experts(sp, it * 2, 1, it * 2 - 1)
                load_experts(sp, it * 2 + 1, 0, it * 2)
            sp.wait_ge(sem("most_known"), 1)
            over_cap = sp.value_load(most_i[0:1, 0:1])
            with sp.If(over_cap > CAP):
                with sp.Fori(NPAIR // 2, ROUNDS * NPAIR // 2) as it:
                    load_experts(sp, it * 2, 1, it * 2 - 1, wrap=True)
                    load_experts(sp, it * 2 + 1, 0, it * 2, wrap=True)
                for j in range(2):
                    sp.wait_ge(sem(f"rows_out{j}"), 16 * (ROUNDS * NPAIR // 2))
            sp.wait_ge(sem("out_stored"), 16 * TC)
            for j in range(2):
                sp.wait_ge(sem(f"rows_out{j}"), 16 * (NPAIR // 2))

        @block.gpsimd
        def _(pool):
            count = [0]

            def step():
                count[0] += 1
                return count[0]

            pool.memset(ones[:], 1.0).then_inc(sem("const_ones"), 1)
            pool.memset(ident[:], 0.0).then_inc(sem("pool_seq"), 1)
            pool.wait_ge(sem("pool_seq"), step())
            pool.affine_select(out=ident[:], in_=ident[:], compare_op=ALU.not_equal, fill=1.0, base=0,
                               pattern=[[-1, P]], channel_multiplier=1).then_inc(sem("const_ident"), 1)
            pool.wait_ge(sem("const_ident"), 1)
            pool.wait_ge(sem("const_ones"), 1)
            pool.affine_select(out=tri[:], in_=ones[:], compare_op=ALU.is_ge, fill=0.0, base=0,
                               pattern=[[1, P]], channel_multiplier=-1).then_inc(sem("const_tri"), 1)
            pool.affine_select(out=stri[:], in_=ones[:], compare_op=ALU.is_gt, fill=0.0, base=0,
                               pattern=[[1, P]], channel_multiplier=-1).then_inc(sem("const_tri"), 1)
            pool.tensor_copy(ident_b[:], ident[:]).then_inc(sem("pool_seq"), 1)
            pool.wait_ge(sem("pool_seq"), step())
            pool.memset(mask_ssd[:], 0.0).then_inc(sem("pool_seq"), 1)
            pool.wait_ge(sem("pool_seq"), step())
            pool.memset(mask_att[:], 0.0).then_inc(sem("pool_seq"), 1)
            pool.wait_ge(sem("pool_seq"), step())
            pool.affine_select(out=mask_ssd[:], in_=mask_ssd[:], compare_op=ALU.is_ge, fill=MASKED, base=0,
                               pattern=[[1, P]], channel_multiplier=-1).then_inc(sem("pool_seq"), 1)
            pool.wait_ge(sem("pool_seq"), step())
            pool.affine_select(out=mask_att[:], in_=mask_att[:], compare_op=ALU.is_ge, fill=MASKED, base=0,
                               pattern=[[-1, P]], channel_multiplier=1).then_inc(sem("pool_seq"), 1)
            pool.wait_ge(sem("pool_seq"), step())
            pool.memset(hsel[:], 0.0).then_inc(sem("pool_seq"), 1)
            pool.wait_ge(sem("pool_seq"), step())
            for part in range(3):
                last = pool.affine_select(out=hsel[:], in_=hsel[:], compare_op=ALU.not_equal, fill=1.0, base=-32 * part,
                                          pattern=[[-1, 32]], channel_multiplier=1)
                if part < 2:
                    last.then_inc(sem("pool_seq"), 1)
                    pool.wait_ge(sem("pool_seq"), step())
            last.then_inc(sem("const_masks"), 1)
            pool.iota(iota[:], [[1, NE]], base=0, channel_multiplier=0, allow_small_or_imprecise_dtypes=True)\
                .then_inc(sem("pool_seq"), 1)
            pool.wait_ge(sem("pool_seq"), step())
            pool.iota(tok[:], [[P, TC]], base=0, channel_multiplier=1, allow_small_or_imprecise_dtypes=True)\
                .then_inc(sem("pool_seq"), 1)
            pool.wait_ge(sem("pool_seq"), step())
            for field in (0, 1, 3):
                for k in range(2):
                    pool.tensor_copy(pay[:, k, :, field], tok[:]).then_inc(sem("tokens_known" if field == 3 and k else "pool_seq"), 1)
                    if field < 3 or k == 0:
                        pool.wait_ge(sem("pool_seq"), step())
            init = m["slot_init"]
            pool.memset(init[:], 0).then_inc(sem("pool_seq"), 1)
            pool.wait_ge(sem("pool_seq"), step())
            pool.memset(init[:].rearrange("p (s w) -> p s w", w=4)[:, :, 1], NO_ROW).then_inc(sem("pool_seq"), 1)
            pool.wait_ge(sem("pool_seq"), step())
            pool.dma_start(slots_dram.rearrange("(p s) w -> p (s w)", p=P), init[:]).then_inc(sem("slots_cleared"), 16)

            def lows(first, end):
                for i in range(first, end, 2):
                    weight_low(pool, i)

            for k in range(0, KC, 2):
                input_low(pool, k)

            def scaled_x(c):
                if c < TC - 1:
                    if c:
                        pool.wait_ge(sem("state_done"), 2 * c)
                    pool.tensor_tensor(heads(Xs[:]), heads(X[:, c, :]), over(dte[:, c, :], P, H, HD), ALU.mult)\
                        .then_inc(sem("x_to_end"), 1)
                if c:
                    pool.wait_ge(sem("gated"), c)
                pool.tensor_tensor(heads(y[:]), heads(X[:, c, :]), over(dskip[:], P, H, HD), ALU.mult)\
                    .then_inc(sem("y_skip"), 1)

            def gate(c):
                pool.wait_ge(sem("y_whole"), 2 * c + 2)
                pool.wait_ge(sem("z_silu"), TC + c + 1)
                pool.tensor_tensor(zs[:, c, :], y[:], zs[:, c, :], ALU.mult).then_inc(sem("gated"), 1)

            lows(0, KC * 5)
            pool.wait_ge(sem("scales_known"), 1)
            pool.wait_ge(sem("x_rows"), 10)
            pool.wait_ge(sem("dskip_in"), 16)
            scaled_x(0)
            lows(KC * 5, KC * 6)
            for c in range(TC - 1):
                gate(c)
                lows(KC * (6 + c), KC * (7 + c))
                scaled_x(c + 1)
            lows(KC * 9, KC * 10)
            gate(TC - 1)
            lows(KC * 10, KC * 10 + HL)
            for k in range(0, KC, 2):
                output_low(pool, k, 0)
            lows(KC * 10 + HL, KC * 13 + HL)
            for k in range(0, KC, 2):
                output_low(pool, k, 1)
            lows(KC * 13 + HL, NSLOT)

            pool.wait_ge(sem("slots_cleared"), 16)
            pool.wait_ge(sem("payload_ready"), 1)
            for k in range(2):
                for c in range(TC):
                    pool.indirect_dma_start(
                        out=slots_dram[:, :], out_offset=bass.IndirectOffsetOnAxis(ap=dest_i[:, k, c:c + 1], axis=0),
                        in_=pay[:, k, c, :], in_offset=None).then_inc(sem("slots_moved"), 16)
            pool.wait_ge(sem("slots_moved"), 16 * (2 * TC))
            pool.wait_ge(sem("xn_out"), 16 * TC)

            def held(n):
                pool.wait_ge(sem("pool_seq"), n + count[0])
                pool.tensor_tensor(spare[0:1, 0:1], ones[0:1, 0:1], ones[0:1, 0:1], ALU.mult).then_inc(sem("pool_seq"), 1)

            def gather(p, r4, n):
                j = r4 % 2
                if r4 >= 2 or not isinstance(p, int):
                    pool.wait_ge(sem("xg_transposed"), p - 1)
                if not isinstance(p, int):
                    pool.wait_ge(sem(f"rows_out{j}"), (p - j) * 8 - 16)
                    pool.wait_ge(sem("y_scaled_act"), p - 3)
                    pool.wait_ge(sem("y_scaled_dve"), p - 3)
                held(n)
                pool.tensor_copy(slot[:, r4, :], slots[:, bass.ds(p, 1), :].rearrange("p a w -> p (a w)"))\
                    .then_inc(sem("pool_seq"), 1)
                held(n + 2)
                pool.indirect_dma_start(out=m["xg"][:, j, :], out_offset=None, in_=xn_dram[:, :],
                                        in_offset=bass.IndirectOffsetOnAxis(ap=slot[:, r4, 0:1], axis=0))\
                    .then_inc(sem(f"xg_in{j}"), 16)

            def gather_more(p, r4, n, row):
                j, e = r4 % 2, p % NPAIR
                pool.wait_ge(sem("xg_transposed"), p - 1)
                pool.wait_ge(sem(f"rows_out{j}"), (p - j) * 8)
                pool.wait_ge(sem("y_scaled_act"), p - 1)
                pool.wait_ge(sem("y_scaled_dve"), p - 1)
                held(n)
                for half in range(2):
                    pool.dma_start(slot[half * CAP:(half + 1) * CAP, r4, :],
                                   slots_by_pos[bass.ds(row, CAP), bass.ds((e + half * NPAIR) * 4, 4)])\
                        .then_inc(sem(f"slot_in{j}"), 16)
                pool.wait_ge(sem(f"slot_in{j}"), (p - j) * 16 - NPAIR * 16 + 32)
                held(n + 1)
                pool.indirect_dma_start(out=m["xg"][:, j, :], out_offset=None, in_=xn_dram[:, :],
                                        in_offset=bass.IndirectOffsetOnAxis(ap=slot[:, r4, 0:1], axis=0))\
                    .then_inc(sem(f"xg_in{j}"), 16)

            def scatter(p, r4, n):
                j = r4 % 2
                if not isinstance(p, int) or p:
                    pool.wait_ge(sem(f"rows_out{1 - j}"), (p + j) * 8)
                pool.wait_ge(sem("y_scaled_act"), p + 1)
                pool.wait_ge(sem("y_scaled_dve"), p + 1)
                held(n)
                pool.indirect_dma_start(out=out[:, :], out_offset=bass.IndirectOffsetOnAxis(ap=slot[:, r4, 1:2], axis=0),
                                        in_=m["yrow"][:, j, :], in_offset=None, bounds_check=T - 1, oob_is_err=False,
                                        compute_op=ALU.add).then_inc(sem(f"rows_out{j}"), 16)

            pool.wait_ge(sem("most_known"), 1)
            for half in range(2):
                pool.dma_start(slots[half * CAP:(half + 1) * CAP, :, :].rearrange("p e w -> p (e w)"),
                               slots_by_pos[0:CAP, half * NPAIR * 4:(half + 1) * NPAIR * 4]).then_inc(sem("slots_moved"), 16)
            pool.wait_ge(sem("slots_moved"), 16 * (2 * TC + 2))
            gather(0, 0, 0)
            gather(1, 1, 3)
            pool.wait_ge(sem("out_stored"), 16 * TC)
            for p in range(2, 4):
                gather(p, p, 4 * p - 2)
                scatter(p - 2, p - 2, 4 * p + 1)
            with pool.Fori(1, NPAIR // 4) as it:
                for r4 in range(4):
                    gather(it * 4 + r4, r4, it * 16 + (4 * r4 - 2))
                    scatter(it * 4 + (r4 - 2), (r4 + 2) % 4, it * 16 + (4 * r4 + 1))
            for p in range(NPAIR - 2, NPAIR):
                scatter(p, p % 4, 3 * NPAIR + p)
            pool.wait_ge(sem("most_known"), 1)
            over_cap = pool.value_load(most_i[0:1, 0:1])
            with pool.If(over_cap > CAP):
                with pool.Fori(NPAIR // 4, ROUNDS * NPAIR // 4) as it:
                    for r4 in (0, 2):
                        for j in range(2):
                            gather_more(it * 4 + (r4 + j), r4 + j, it * 12 + (NPAIR + 3 * r4 + 2 * j), (it // (NPAIR // 4)) * CAP)
                        for j in range(2):
                            scatter(it * 4 + (r4 + j), r4 + j, it * 12 + (NPAIR + 3 * r4 + 4 + j))
                for j in range(2):
                    pool.wait_ge(sem(f"rows_out{j}"), 16 * (ROUNDS * NPAIR // 2))

        @block.scalar
        def _(act):
            def rstd(total, ln, r, name, scale, width):
                act.activation(ln, total, ACT.Ln, bias=eps[:], scale=1.0 / width).then_inc(sem(name + "_ln"), 1)
                act.wait_ge(sem(name + "_ln"), scale)
                act.activation(r, ln, ACT.Exp, scale=-0.5).then_inc(sem(name + "_rstd"), 1)

            act.preload_act_table_set("natural_log_exp_and_others")
            act.wait_ge(sem("eps_set"), 1)
            for c in range(TC):
                act.wait_ge(sem(f"x_in{c}"), 16)
                if c:
                    act.wait_ge(sem("x_squared"), c)
                act.activation(hTf[:, 0:2, :].rearrange("p k t -> p (k t)"), xin[:, c, :], ACT.Square, accum_out=ssq[:, c:c + 1])\
                    .then_inc(sem("x_squared"), 1)
            act.wait_ge(sem("x_squared"), TC)
            rstd(ssq[:], rln[:], rx[:], "x", 1, D)
            act.dma_start(brow[:, 0:H], dt_bias[0].partition_broadcast(P)).then_inc(sem("brow_in"), 16)
            act.dma_start(brow[:, H:], fox_f_bias[0].partition_broadcast(P)).then_inc(sem("brow_in"), 16)
            act.dma_start(alog[:], a_log[0].partition_broadcast(P)).then_inc(sem("alog_in"), 16)
            act.dma_start(dskip[:], d_skip[0].partition_broadcast(P)).then_inc(sem("dskip_in"), 16)
            act.dma_start(rbias[:, 0:NG], b_router_group[0].partition_broadcast(P)).then_inc(sem("rbias_in"), 16)
            act.dma_start(rbias[:, NG:], b_router_expert[0].partition_broadcast(P)).then_inc(sem("rbias_in"), 16)
            for k in range(KC):
                act.wait_ge(sem("hT_scaled"), k + 1)
                act.activation(hTh[:, k, :], hTf[:, k, :], ACT.Copy).then_inc(sem("hT_high"), 1)

            def high(i):
                act.wait_ge(sem(f"raw_in{i % RAW}"), 16 * (i // RAW + 1))
                if i >= HL:
                    slot_read(act, i - HL)
                act.activation(wh[:, i % HL, :], raw[:, i % RAW, :], ACT.Copy).then_inc(sem("w_high"), 1)

            for i in range(HL):
                high(i)

            act.wait_ge(sem("dt_abs"), 1)
            act.activation(ew[:], ab[:], ACT.Exp, scale=-1.0).then_inc(sem("dt_exp"), 1)
            act.wait_ge(sem("alog_in"), 16)
            act.activation(ea[:], alog[:], ACT.Exp).then_inc(sem("a_exp"), 1)
            act.wait_ge(sem("dt_one_plus"), 1)
            act.activation(ab[:], w1[:], ACT.Ln).then_inc(sem("dt_ln"), 1)
            def highs_after(n):
                for i in slots_after(n):
                    high(i)

            def silu_x(n):
                act.wait_ge(sem("conv_done"), n + 1)
                f = FEAT[n]
                if f < 8:
                    if n >= 6:
                        act.wait_ge(sem("x_transposed"), n - 2 - 1)
                    dst = xs[:, n % 2, :]
                else:
                    dst = BC[:, f - 8, :]
                act.activation(dst, acc[:, n % 2, :], ACT.Silu).then_inc(sem("x_silu"), 1)

            for n in range(N_XBC, N_Z):
                act.wait_ge(sem("pass_done"), n + 1)
                if n >= 2:
                    act.wait_ge(sem("conv_done"), n - 1)
                act.activation(up[:, n % 2, 3:], ps[n % 2][:], ACT.Copy).then_inc(sem("up_copied"), 1)
                if n:
                    silu_x(n - 1)
                highs_after(n)
            silu_x(N_Z - 1)
            act.wait_ge(sem("ends_known"), 1)
            act.activation(ecum[:], cum[:, :, 0:H], ACT.Exp).then_inc(sem("decays_exp"), 1)
            act.activation(dte[:], res[:, :, 0:H], ACT.Exp).then_inc(sem("decays_exp"), 1)
            act.activation(etot[:], tot[:, :, 0:H], ACT.Exp).then_inc(sem("decays_exp"), 1)
            for n in range(N_Z, N_QK):
                i = n - N_Z
                act.wait_ge(sem("pass_done"), n + 1)
                act.activation(zs[:, n % 4, (i // 4) * BLK:(i // 4 + 1) * BLK], ps[n % 2][:], ACT.Silu)\
                    .then_inc(sem("z_silu"), 1)
                highs_after(n)

            def qk_square(i):
                act.wait_ge(sem("pass_done"), N_QK + i + 1)
                if i:
                    act.wait_ge(sem("qk_sum"), i)
                act.activation(m["sq"][:], ps[i % 2][:], ACT.Square).then_inc(sem("qk_squared"), 1)

            def qk_rstd(i):
                act.wait_ge(sem("qk_sum"), i + 1)
                rstd(qss[:, i, :], qss[:, i, :], qr[:, i, :], "qk", i + 1, HD)

            def qk_store(i):
                act.wait_ge(sem("qk_transposed"), i + 1)
                b, c = (i // 4) % 2, i % 4
                dst = (qT if i < 8 else kT)[:, 4 * b:4 * b + 4, c * P:(c + 1) * P]
                src = tbank(T_QK + i)[:].rearrange("p (r t) -> p r t", r=4)
                act.activation(dst, src, ACT.Copy, scale=qkw[:] if i < 8 else 1.0).then_inc(sem("qkT_stored"), 1)

            def decays(c, w):
                act.wait_ge(sem("seg_done"), 4 * c + w + 1)
                if 4 * c + w >= 2:
                    act.wait_ge(sem("m_done"), 4 * c + w - 1)
                for h in range(4 * w, 4 * w + 4):
                    q = (h % 4) * P
                    last = act.activation(dec[:, w % 2, q:q + P], ps[5 + w % 2][:, q:q + P], ACT.Exp, bias=ncum[:, c, h:h + 1])
                last.then_inc(sem("decay_exp"), 1)

            def cb_copy(c):
                act.wait_ge(sem("cb_done"), c + 1)
                if c:
                    act.wait_ge(sem("m_done"), 4 * c)
                act.activation(cbs[:], ps[4][:, 0:256], ACT.Copy).then_inc(sem("cb_copied"), 1)

            def y_square(c):
                act.wait_ge(sem("gated"), c + 1)
                act.activation(Pe[:, 0:2, :].rearrange("p a t -> p (a t)"), zs[:, c, :], ACT.Square, accum_out=yss[:, c:c + 1]).then_inc(sem("y_squared"), 1)
                act.wait_ge(sem("y_squared"), c + 1)

            act.preload_act_table_set("natural_log_exp_and_others")
            for i in range(16):
                n = N_QK + i
                qk_square(i)
                qk_rstd(i)
                if i:
                    qk_store(i - 1)
                if i % 4 == 0:
                    cb_copy(i // 4)
                    decays(i // 4, 0)
                    decays(i // 4, 1)
                if i % 4 == 1:
                    decays(i // 4, 2)
                    decays(i // 4, 3)
                highs_after(n)
            qk_store(15)
            def y_high(k, group):
                act.wait_ge(sem("yT_scaled"), group * KC + k + 1)
                if k == 0:
                    act.wait_ge(sem("gated"), TC)
                    if group:
                        act.wait_ge(sem("pass_done"), N_AO)
                hi = (m["syTh"], m["ayTh"])[group]
                act.activation(hi[:, k, :], yTf[:, k % 2, :], ACT.Copy).then_inc(sem("yT_high"), 1)

            for i in range(8):
                n = N_V + i
                act.wait_ge(sem("pass_done"), n + 1)
                if i == 0:
                    act.wait_ge(sem("diag_done"), 4 * TC)
                    act.wait_ge(sem("y_skip"), TC)
                act.activation(V[:, i % 4, (i // 4) * BLK:(i // 4 + 1) * BLK], ps[n % 2][:], ACT.Copy).then_inc(sem("v_copied"), 1)
                highs_after(n)
                for k in SSD_OUT.get(i, ()):
                    y_high(k, 0)
                if i == 5:
                    for c in range(TC):
                        y_square(c)
                    rstd(yss[:], yln[:], rs_s[:], "y", 1, DS)

            for n in range(N_SO, N_AO):
                act.wait_ge(sem("pass_done"), n + 1)
                highs_after(n)

            def p_exp(v):
                n = P * (v // H + 1)
                act.wait_ge(sem("max_known"), v + 1)
                if v >= 3:
                    act.wait_ge(sem("p_transposed"), v - 2)
                act.activation(Pe[:, v % 3, 0:n], ps[4 + v % 3][:, 0:n], ACT.Exp, bias=nmax[:, v:v + 1],
                               accum_out=rsum[:, v:v + 1]).then_inc(sem("p_exp"), 1)

            def pt_store(v):
                n = P * (v // H + 1)
                act.wait_ge(sem("p_transposed"), v + 1)
                if v >= 2:
                    act.wait_ge(sem("pv_done"), v - 1)
                act.activation(PT[:, v % 2, 0:n], tbank(T_P + v)[:, 0:n], ACT.Copy).then_inc(sem("pt_stored_act"), 1)

            act.wait_ge(sem("slots_cleared"), 16)
            for v in range(NU + 1):
                if v < NU:
                    p_exp(v)
                if v >= 1 and (v - 1) % 2 == 0:
                    pt_store(v - 1)
            act.preload_act_table_set("natural_log")
            for c in range(TC):
                act.wait_ge(sem("ya_stored"), 2 * c + 2)
                if c:
                    act.wait_ge(sem("ya_squared"), c)
                else:
                    act.wait_ge(sem("p_transposed"), NU)
                act.activation(Pe[:, 0:2, :].rearrange("p a t -> p (a t)"), ya[:, c, :], ACT.Square, accum_out=ass[:, c:c + 1]).then_inc(sem("ya_squared"), 1)
            act.wait_ge(sem("ya_squared"), TC)
            rstd(ass[:], aln[:], rs_a[:], "ya", 1, DS)
            for k in range(KC):
                if k == 0:
                    act.wait_ge(sem("s_done"), NU)
                y_high(k, 1)
            for n in range(N_AO, N_AO + 4):
                act.wait_ge(sem("pass_done"), n + 1)
                highs_after(n)

            act.preload_act_table_set("natural_log")
            act.dma_start(m["wffn"][:], norm_ffn_w[0].partition_broadcast(P)).then_inc(sem("wffn_in"), 16)
            act.dma_start(wr[:, :, 0:NG], w_router_group[0].rearrange("(k p) g -> p k g", p=P)).then_inc(sem("wr_in"), 16)
            act.dma_start(wr[:, :, NG:], w_router_expert[0].rearrange("(k p) g -> p k g", p=P)).then_inc(sem("wr_in"), 16)
            for c in range(TC):
                act.wait_ge(sem("residual_added"), 12 + c + 1)
                if c:
                    act.wait_ge(sem("f_squared"), c)
                act.activation(m["xnT"][:, 0:2, :].rearrange("p k t -> p (k t)"), zs[:, c, :], ACT.Square, accum_out=fss[:, c:c + 1]).then_inc(sem("f_squared"), 1)
            act.wait_ge(sem("f_squared"), TC)
            rstd(fss[:], fln[:], rf[:], "f", 1, D)
            for c in range(TC):
                act.wait_ge(sem("xn_scaled"), c + 1)
                act.dma_start(xn_dram[c * P:(c + 1) * P, :], xn[:, c, :]).then_inc(sem("xn_out"), 16)
            for k in range(0, KC, 2):
                act.wait_ge(sem("xn_transposed"), k + 1)
                act.activation(m["xnT"][:, k, :], tbank(T_XN + k)[:], ACT.Copy).then_inc(sem("xnT_stored_act"), 1)
            act.wait_ge(sem("router_done"), 1)
            act.activation(lgT[HD:HD + NG + NE, :], ps[4][HD:HD + NG + NE, 0:T // 2], ACT.Copy).then_inc(sem("logits_copied"), 1)
            act.wait_ge(sem("group_shifted"), 1)
            act.activation(gex[:], gex[:], ACT.Exp).then_inc(sem("group_exp"), 1)
            act.wait_ge(sem("pair_diff"), 1)
            act.activation(e2, e2, ACT.Exp).then_inc(sem("pair_exp"), 1)

            def expert(p, r4, first=False):
                j = r4 % 2
                act.wait_ge(sem("xg_transposed"), p + 1)
                if not first:
                    act.wait_ge(sem("gate_up_done"), p - 1)
                act.activation(m["xgT"][:, j, 0:4, :].rearrange("p k t -> p (k t)"), ps[2][:], ACT.Copy).then_inc(sem("xgT_act"), 1)
                act.wait_ge(sem("gate_up_done"), p + 1)
                if not first or j:
                    act.wait_ge(sem("hid_done"), p)
                act.activation(m["sg"][:], ps[j][:, 0:DE], ACT.Silu).then_inc(sem("gate_silu"), 1)
                act.wait_ge(sem("down_done"), p + 1)
                if not first:
                    act.wait_ge(sem(f"rows_out{j}"), (p - j) * 8)
                act.activation(m["yrow"][:, j, 0:BLK], ps[6][:], ACT.Copy, scale=slot[:, r4, 2:3].bitcast(F32))\
                    .then_inc(sem("y_scaled_act"), 1)

            experts(act, expert)

        @block.tensor
        def _(pe):
            pe.wait_ge(sem("const_ident"), 1)
            pe.wait_ge(sem("vec_in"), 16 * 9)
            pe.transpose(ps[7][:, 0:CV_N], vecs[:], ident[0:CV_N, 0:CV_N]).then_inc(sem("cvec_done"), 1)
            for k in range(KC):
                if k >= 2:
                    t_read(pe, k - 2)
                for c in range(TC):
                    pe.wait_ge(sem("x_scaled"), c + 1)
                    last = pe.transpose(tbank(k)[:, c * P:(c + 1) * P], xin[:, c, k * P:(k + 1) * P], ident[:])
                last.then_inc(sem("hT_done"), 1)
            pe.wait_ge(sem("wdtf_in"), 16 * 2)
            for k in range(KC):
                pe.wait_ge(sem("hT_scaled"), k + 1)
                for half in range(2):
                    last = pe.matmul(ps[5][half * HD:half * HD + 32, 0:T // 2], wdtf[:, k, :],
                                     hTf[:, k, half * T // 2:(half + 1) * T // 2], start=(k == 0), stop=(k == KC - 1))
            last.then_inc(sem("dtf_done"), 1)

            def three(dst, ah, al, bh, bl, start, stop):
                pe.matmul(dst, ah, bh, start=start, stop=False)
                pe.matmul(dst, ah, bl, start=False, stop=False)
                return pe.matmul(dst, al, bh, start=False, stop=stop)

            def one_pass(n):
                b, j = divmod(n, 4)
                kind = BLOCKS[b][0]
                if n >= 2 and n not in (N_AO, N_AO + 1):
                    pass_read(pe, n - 2)
                if n in (N_AO, N_AO + 1):
                    pe.wait_ge(sem("ya_stored"), 6 + n - N_AO + 1)
                hi, lo = {"ao": (m["ayTh"], m["ayTl"]), "so": (m["syTh"], m["syTl"])}.get(kind, (hTh, hTl))
                for k in range(KC):
                    i = b * KC + k
                    if j == 0:
                        low_made(pe, "w", i)
                        if kind == "so":
                            low_made(pe, "yT", k)
                        elif kind == "ao":
                            low_made(pe, "yT", KC + k)
                        elif n == 0:
                            low_made(pe, "hT", k)
                    s = i % HL
                    if kind == "xbc":
                        f = slice(j * P, (j + 1) * P)
                        last = three(ps[n % 2][:], wh[:, s, f], wl[:, s, f], hTh[:, k, :], hTl[:, k, :], k == 0, k == KC - 1)
                    else:
                        t = slice(j * P, (j + 1) * P)
                        last = three(ps[n % 2][:], hi[:, k, t], lo[:, k, t], wh[:, s, :], wl[:, s, :], k == 0, k == KC - 1)
                    if j == 3 and k < KC - 1:
                        last.then_inc(sem("slot_used"), 1)
                last.then_inc(sem("pass_done"), 1)

            def x_transpose(q):
                n = TRANSPOSED[q]
                f = FEAT[n]
                pe.wait_ge(sem("x_silu"), n + 1)
                t_read(pe, T_X + q - 2)
                src = xs[:, n % 2, :] if f < 8 else BC[:, f - 8, :]
                for c in range(TC):
                    last = pe.transpose(tbank(T_X + q)[:, c * P:(c + 1) * P], src[:, c * P:(c + 1) * P], ident[:])
                last.then_inc(sem("x_transposed"), 1)

            def small_sums():
                pe.wait_ge(sem("dtf_copied"), 2)
                for c in range(TC):
                    at = slice(c // 2 * HD, c // 2 * HD + 32)
                    last = pe.transpose(ps[6 + c // 2][:, c % 2 * 32:(c % 2 + 1) * 32], m["dtfT"][at, c % 2 * P:(c % 2 + 1) * P],
                                        ident[at, at])
                last.then_inc(sem("dtf_rows"), 1)

            def small_cums():
                pe.wait_ge(sem("logs_known"), 1)
                pe.wait_ge(sem("const_tri"), 2)
                pe.wait_ge(sem("const_ones"), 1)
                flat = lf[:].rearrange("p c h -> p (c h)")
                pe.matmul(ps[7][:, 0:P], tri[:], flat, start=True, stop=True)
                pe.matmul(ps[7][:, P:2 * P], ones[:], flat, start=True, stop=True).then_inc(sem("cums_done"), 1)

            def small_rows():
                pe.wait_ge(sem("parts_known"), 1)
                pe.wait_ge(sem("const_masks"), 1)
                for c in range(TC):
                    last = pe.transpose(ps[5][0:96, :].bitcast(BF16)[:, c * P:(c + 1) * P], cb3[:, c, :], ident_b[:])
                last.then_inc(sem("crow_done"), 1)

            tr = 0
            for n in range(N_QK):
                one_pass(n)
                if n == 0:
                    small_sums()
                if n == 1:
                    small_cums()
                if n == 2:
                    small_rows()
                while tr < 10 and TRANSPOSED[tr] <= n - 2:
                    x_transpose(tr)
                    tr += 1

            def seg(c, w):
                v = 4 * c + w
                if v >= 2:
                    pe.wait_ge(sem("decay_exp"), v - 1)
                for h in range(4 * w, 4 * w + 4):
                    dst = ps[5 + w % 2][:, (h % 4) * P:(h % 4 + 1) * P]
                    pe.matmul(dst, hsel[:, h:h + 1].broadcast_to([96, P]), crow[:, c * P:(c + 1) * P], start=True, stop=False)
                    last = pe.matmul(dst, ident_b[:], mask_ssd[:], start=False, stop=True)
                last.then_inc(sem("seg_done"), 1)

            def diag(c, w):
                pe.wait_ge(sem("m_done"), 4 * c + w + 1)
                g = w // 2
                if w % 2 == 0:
                    if g:
                        pe.wait_ge(sem("y_diag"), 2 * c + 1)
                    elif c:
                        pe.wait_ge(sem("state_kept"), 2 * c)
                for h in range(4 * w, 4 * w + 4):
                    at = (h % 8) * HD
                    n = P if h % 8 < 7 else HD
                    last = pe.matmul(ps[7][:, at:at + n], M[:, w % 2, (h % 4) * P:(h % 4 + 1) * P], X[:, c, h * HD:h * HD + n],
                                     start=True, stop=True)
                last.then_inc(sem("diag_done"), 1)

            def cb(c):
                if c:
                    pe.wait_ge(sem("state_kept"), 2 * c - 1)
                for g in range(2):
                    last = pe.matmul(ps[4][:, g * P:(g + 1) * P], BC[:, g, c * P:(c + 1) * P], BC[:, 2 + g, c * P:(c + 1) * P],
                                     start=True, stop=True)
                last.then_inc(sem("cb_done"), 1)

            def y_off(c, g):
                if g == 0:
                    pe.wait_ge(sem("cb_copied"), c + 1)
                else:
                    pe.wait_ge(sem("y_off_scaled"), 2 * (c - 1) + 1)
                pe.wait_ge(sem("state_kept"), 2 * (c - 1) + g + 1)
                pe.matmul(ps[4][:], BC[:, 2 + g, c * P:(c + 1) * P], Hst[:, g * BLK:(g + 1) * BLK], start=True, stop=True)\
                    .then_inc(sem("y_off_done"), 1)

            def state(c, g):
                pe.wait_ge(sem("x_to_end"), c + 1)
                if g == 0:
                    if c:
                        pe.wait_ge(sem("y_off_scaled"), 2 * c)
                    else:
                        pe.wait_ge(sem("cb_copied"), 1)
                else:
                    pe.wait_ge(sem("y_diag"), 2 * c + 2)
                pe.matmul(ps[4 if g == 0 else 7][:], Btm[:, c, g * P:(g + 1) * P], Xs[:, g * BLK:(g + 1) * BLK],
                          start=True, stop=True).then_inc(sem("state_done"), 1)

            def qk_transpose(i):
                pe.wait_ge(sem("qk_scaled"), i + 1)
                t_read(pe, T_QK + i - 2)
                for r in range(4):
                    last = pe.transpose(tbank(T_QK + i)[:, r * P:(r + 1) * P], m["qn"][:, i % 2, r * P:(r + 1) * P], ident[:])
                last.then_inc(sem("qk_transposed"), 1)

            pe.wait_ge(sem("crow_copied"), 1)
            for i in range(17):
                if i < 16:
                    one_pass(N_QK + i)
                else:
                    one_pass(N_V)
                if i >= 1:
                    qk_transpose(i - 1)
                if i == 0:
                    cb(0)
                    seg(0, 0)
                    seg(0, 1)
                    continue
                c, step = (i - 1) // 4, (i - 1) % 4
                if step == 0:
                    diag(c, 0)
                    diag(c, 1)
                    seg(c, 2)
                    seg(c, 3)
                    if c:
                        y_off(c, 0)
                if step == 1:
                    if c:
                        y_off(c, 1)
                    diag(c, 2)
                    diag(c, 3)
                if step == 2 and c < TC - 1:
                    state(c, 0)
                    state(c, 1)
                if step == 3 and c < TC - 1:
                    cb(c + 1)
                    seg(c + 1, 0)
                    seg(c + 1, 1)
            def y_transpose(k, group):
                i = (T_SY, T_AY)[group] + k
                t_read(pe, i - 2)
                src = (zs, ya)[group]
                for c in range(TC):
                    if group == 0:
                        pe.wait_ge(sem("gated"), c + 1)
                    last = pe.transpose(tbank(i)[:, c * P:(c + 1) * P], src[:, c, k * P:(k + 1) * P], ident[:])
                last.then_inc(sem("sy_transposed" if group == 0 else "ay_transposed"), 1)

            for n in range(N_V + 1, N_SO):
                one_pass(n)
                for k in SSD_OUT.get(n - N_V, ()):
                    y_transpose(k, 0)

            for n in range(N_SO, N_AO):
                one_pass(n)

            def scores(v):
                qb, h = divmod(v, H)
                n = P * (qb + 1)
                if v >= 3:
                    pe.wait_ge(sem("p_exp"), v - 2)
                r = slice((h % 2) * HD, (h % 2 + 1) * HD)
                s = ps[4 + v % 3]
                pe.matmul(s[:, 0:n], qT[r, h // 2, qb * P:(qb + 1) * P], kT[r, h // 2, 0:n], start=True, stop=False)
                pe.matmul(s[:, 0:n], hsel[:, H + h:H + h + 1].broadcast_to([96, P]), crow[:, 0:n], start=False, stop=True)
                pe.matmul(s[:, qb * P:n], ident_b[:], mask_att[:], start=False, stop=True, skip_group_check=True)\
                    .then_inc(sem("s_done"), 1)

            def p_transpose(v):
                pe.wait_ge(sem("p_exp"), v + 1)
                t_read(pe, T_P + v - 2)
                for kb in range(v // H + 1):
                    last = pe.transpose(tbank(T_P + v)[:, kb * P:(kb + 1) * P], Pe[:, v % 3, kb * P:(kb + 1) * P], ident[:])
                last.then_inc(sem("p_transposed"), 1)

            def pv(v):
                qb, h = divmod(v, H)
                pt_stored(pe, v)
                w = v // 8
                if v % 8 == 0:
                    if w >= 2:
                        pe.wait_ge(sem("ya_stored"), w - 1)
                    else:
                        pe.wait_ge(sem("residual_added"), 6 + w + 1)
                at = (h % 8) * HD
                n = P if h % 8 < 7 else HD
                for kb in range(qb + 1):
                    last = pe.matmul(ps[w % 2][:, at:at + n], PT[:, v % 2, kb * P:(kb + 1) * P], V[:, kb, h * HD:h * HD + n],
                                     start=(kb == 0), stop=(kb == qb))
                last.then_inc(sem("pv_done"), 1)

            pe.wait_ge(sem("v_copied"), 8)
            pe.wait_ge(sem("qkT_stored"), 16)
            for v in range(NU + 3):
                if v < NU:
                    scores(v)
                if 1 <= v <= NU:
                    p_transpose(v - 1)
                if v >= 3:
                    pv(v - 3)
            pe.wait_ge(sem("ya_stored"), 8)
            for k in range(KC):
                y_transpose(k, 1)
            for n in range(N_AO, N_END):
                one_pass(n)

            def router(k):
                xnT_stored(pe, k)
                for half in range(2):
                    last = pe.matmul(ps[4][half * HD:half * HD + NG + NE, 0:T // 2], wr[:, k, :],
                                     m["xnT"][:, k, half * T // 2:(half + 1) * T // 2], start=(k == 0), stop=(k == KC - 1))
                return last

            pe.wait_ge(sem("wr_in"), 16 * 2)
            for k in range(KC + 2):
                if k < KC:
                    t_read(pe, T_XN + k - 2)
                    for c in range(TC):
                        pe.wait_ge(sem("xn_scaled"), c + 1)
                        last = pe.transpose(tbank(T_XN + k)[:, c * P:(c + 1) * P], xn[:, c, k * P:(k + 1) * P], ident[:])
                    last.then_inc(sem("xn_transposed"), 1)
                if k >= 2:
                    last = router(k - 2)
            last.then_inc(sem("router_done"), 1)
            pe.wait_ge(sem("logits_copied"), 2)
            for c in range(TC):
                r = slice(c // 2 * HD, c // 2 * HD + NG + NE)
                last = pe.transpose(ps[5 + c // 2][:, c % 2 * 36:(c % 2 + 1) * 36], lgT[r, c % 2 * P:(c % 2 + 1) * P], ident[r, r])
            last.then_inc(sem("router_rows"), 1)
            pe.wait_ge(sem("occupied"), 1)
            flat = occ[:].rearrange("p c e -> p (c e)")
            last = pe.matmul(ps[7][:, 0:P], stri[:], flat, start=True, stop=True)
            for c in range(1, TC):
                last = pe.matmul(ps[7][:, c * NE:P], ones[:], flat[:, 0:P - c * NE], start=False, stop=True,
                                 skip_group_check=True)
            last.then_inc(sem("ranks_done"), 1)
            for c in range(TC):
                last = pe.matmul(ps[6][:, 0:NE], ones[:], occ[:, c, :], start=(c == 0), stop=(c == TC - 1))
            last.then_inc(sem("ranks_done"), 1)

            def expert(p, r4, first=False):
                j = r4 % 2
                pe.wait_ge(sem(f"xg_in{j}"), (p - j) * 8 + 16)
                if not first or j:
                    pe.wait_ge(sem("xgT_act"), p)
                    pe.wait_ge(sem("xgT_dve"), p)
                for k in range(KC):
                    last = pe.transpose(ps[2 + k // 4][:, (k % 4) * P:(k % 4 + 1) * P], m["xg"][:, j, k * P:(k + 1) * P], ident[:])
                last.then_inc(sem("xg_transposed"), 1)
                b, had = gate_up_buffer(p, r4)
                db, dhad = down_buffer(p, r4)
                pe.wait_ge(sem(f"gu_in{b}"), had * 32)
                pe.wait_ge(sem("xgT_act"), p + 1)
                pe.wait_ge(sem("xgT_dve"), p + 1)
                if not first:
                    pe.wait_ge(sem("hid_done"), p - 1)
                gu, dn = m[f"gu{b}"], m[f"dn{db}"]
                for k in range(KC):
                    for half in range(2):
                        r = slice(half * CAP, (half + 1) * CAP)
                        last = pe.matmul(ps[j][r, :].rearrange("p (w f) -> p w f", w=2), m["xgT"][:, j, k, r],
                                         gu[:, half, :, k, :], start=(k == 0), stop=(k == KC - 1))
                last.then_inc(sem("gate_up_done"), 1)
                pe.wait_ge(sem("hid_done"), p + 1)
                if not first or j:
                    pe.wait_ge(sem("hidT_stored"), p)
                for q in range(2):
                    last = pe.transpose(ps[4][:, q * P:(q + 1) * P], m["hid"][:, q * P:(q + 1) * P], ident[:])
                last.then_inc(sem("hid_transposed"), 1)
                pe.wait_ge(sem("hidT_stored"), p + 1)
                pe.wait_ge(sem(f"dn_in{db}"), dhad * 16)
                if not first or j:
                    pe.wait_ge(sem("y_scaled_act"), p)
                    pe.wait_ge(sem("y_scaled_dve"), p)
                for nb in range(2):
                    for q in range(2):
                        for half in range(2):
                            r = slice(half * CAP, (half + 1) * CAP)
                            at = q * P + half * CAP
                            last = pe.matmul(ps[6 + nb][r, :], m["hidT"][:, j, at:at + CAP], dn[:, half, q, nb * BLK:(nb + 1) * BLK],
                                             start=(q == 0), stop=(q == 1))
                last.then_inc(sem("down_done"), 1)

            experts(pe, expert)

        @block.vector
        def _(dve):
            count = [0]

            def step():
                count[0] += 1
                return count[0]

            dve.memset(eps[:], EPS).then_inc(sem("eps_set"), 1)
            dve.wait_ge(sem("eps_set"), 1)
            dve.memset(up[:, :, 0:3], 0.0).then_inc(sem("dve_seq"), 1)
            dve.wait_ge(sem("dve_seq"), step())
            dve.wait_ge(sem("cvec_done"), 1)
            dve.tensor_copy(cvec[:], ps[7][:, 0:CV_N]).then_inc(sem("cvec_copied"), 1)
            dve.wait_ge(sem("cvec_copied"), 1)
            dve.scalar_tensor_tensor(out=qkw[:], in0=cvec[:, CV_Q:CV_Q + 1], scalar=HD ** -0.5, in1=cvec[:, CV_K:CV_K + 1],
                                     op0=ALU.mult, op1=ALU.mult).then_inc(sem("qkw_known"), 1)
            dve.wait_ge(sem("qkw_known"), 1)
            dve.wait_ge(sem("x_rstd"), 1)
            for c in range(TC):
                dve.tensor_scalar(xin[:, c, :], xin[:, c, :], rx[:, c:c + 1], None, ALU.mult).then_inc(sem("x_scaled"), 1)
            for k in range(KC):
                dve.wait_ge(sem("hT_done"), k + 1)
                dve.tensor_scalar(hTf[:, k, :], tbank(k)[:], cvec[:, CV_MIX + k:CV_MIX + k + 1], None, ALU.mult)\
                    .then_inc(sem("hT_scaled"), 1)
            for k in range(1, KC, 2):
                input_low(dve, k)
            for i in range(1, HL, 2):
                weight_low(dve, i)
            dve.wait_ge(sem("dtf_done"), 1)
            for half in range(2):
                at = slice(half * HD, half * HD + 32)
                dve.tensor_copy(m["dtfT"][at, :], ps[5][at, 0:T // 2]).then_inc(sem("dtf_copied"), 1)
            dve.wait_ge(sem("dtf_rows"), 1)
            dve.wait_ge(sem("brow_in"), 16 * 2)
            for half in range(2):
                dve.tensor_tensor(u[:, 2 * half:2 * half + 2, :], ps[6 + half][:, 0:HD].rearrange("p (c h) -> p c h", c=2),
                                  brow[:].unsqueeze(1).broadcast_to([P, 2, 32]), ALU.add).then_inc(sem("dve_seq"), 1)
                last = step()
            dve.wait_ge(sem("dve_seq"), last)
            dve.tensor_scalar(u[:, :, H:], u[:, :, H:], -1.0, None, ALU.mult).then_inc(sem("dve_seq"), 1)
            dve.wait_ge(sem("dve_seq"), step())
            dve.scalar_tensor_tensor(out=ab[:], in0=u[:], scalar=-1.0, in1=u[:], op0=ALU.mult, op1=ALU.max)\
                .then_inc(sem("dt_abs"), 1)
            dve.wait_ge(sem("dt_abs"), 1)
            dve.wait_ge(sem("dt_exp"), 1)
            dve.tensor_scalar(w1[:], ew[:], 1.0, None, ALU.add).then_inc(sem("dt_one_plus"), 1)
            dve.wait_ge(sem("dt_one_plus"), 1)
            dve.reciprocal(rw[:], w1[:]).then_inc(sem("dve_seq"), 1)
            dve.wait_ge(sem("dve_seq"), step())
            dve.scalar_tensor_tensor(out=cor[:], in0=w1[:], scalar=-1.0, in1=ew[:], op0=ALU.add, op1=ALU.subtract)\
                .then_inc(sem("dve_seq"), 1)
            dve.wait_ge(sem("dve_seq"), step())
            dve.tensor_tensor(cor[:], cor[:], rw[:], ALU.mult).then_inc(sem("dve_seq"), 1)
            dve.wait_ge(sem("dve_seq"), step())
            dve.wait_ge(sem("dt_ln"), 1)
            dve.tensor_tensor(sp[:], ab[:], cor[:], ALU.subtract).then_inc(sem("dve_seq"), 1)
            dve.wait_ge(sem("dve_seq"), step())
            dve.scalar_tensor_tensor(out=sp[:], in0=u[:], scalar=0.0, in1=sp[:], op0=ALU.max, op1=ALU.add)\
                .then_inc(sem("dve_seq"), 1)
            dve.wait_ge(sem("dve_seq"), step())
            dve.wait_ge(sem("a_exp"), 1)
            dve.scalar_tensor_tensor(out=lf[:, :, 0:H], in0=sp[:, :, 0:H], scalar=-1.0,
                                     in1=ea[:].unsqueeze(1).broadcast_to([P, TC, H]), op0=ALU.mult, op1=ALU.mult)\
                .then_inc(sem("dve_seq"), 1)
            dve.wait_ge(sem("dve_seq"), step())
            dve.tensor_scalar(lf[:, :, H:], sp[:, :, H:], -1.0, None, ALU.mult).then_inc(sem("logs_known"), 1)
            dve.wait_ge(sem("logs_known"), 1)
            dve.wait_ge(sem("cums_done"), 1)
            dve.tensor_copy(cum[:], ps[7][:, 0:P].rearrange("p (c h) -> p c h", c=TC)).then_inc(sem("dve_seq"), 1)
            dve.wait_ge(sem("dve_seq"), step())
            dve.tensor_copy(tot[:], ps[7][:, P:2 * P].rearrange("p (c h) -> p c h", c=TC)).then_inc(sem("dve_seq"), 1)
            dve.wait_ge(sem("dve_seq"), step())
            for c in range(TC - 1):
                dve.tensor_tensor(cum[:, c + 1:, H:], cum[:, c + 1:, H:],
                                  tot[:, c:c + 1, H:].broadcast_to([P, TC - 1 - c, H]), ALU.add).then_inc(sem("dve_seq"), 1)
                dve.wait_ge(sem("dve_seq"), step())
            dve.tensor_scalar(cum[:, :, H:], cum[:, :, H:], -1.0, None, ALU.mult).then_inc(sem("dve_seq"), 1)
            dve.wait_ge(sem("dve_seq"), step())
            dve.tensor_scalar(ncum[:], cum[:, :, 0:H], -1.0, None, ALU.mult).then_inc(sem("dve_seq"), 1)
            dve.wait_ge(sem("dve_seq"), step())
            dve.tensor_tensor(res[:, :, 0:H], tot[:, :, 0:H], cum[:, :, 0:H], ALU.subtract).then_inc(sem("ends_known"), 1)
            dve.wait_ge(sem("ends_known"), 1)
            dve.tensor_copy(cb3[:, :, 0:32], cum[:]).then_inc(sem("dve_seq"), 1)
            dve.wait_ge(sem("dve_seq"), step())
            dve.tensor_tensor(u[:], cum[:], cb3[:, :, 0:32], ALU.subtract).then_inc(sem("dve_seq"), 1)
            dve.wait_ge(sem("dve_seq"), step())
            dve.tensor_copy(cb3[:, :, 32:64], u[:]).then_inc(sem("dve_seq"), 1)
            dve.wait_ge(sem("dve_seq"), step())
            dve.tensor_tensor(u[:], u[:], cb3[:, :, 32:64], ALU.subtract).then_inc(sem("dve_seq"), 1)
            dve.wait_ge(sem("dve_seq"), step())
            dve.tensor_copy(cb3[:, :, 64:96], u[:]).then_inc(sem("parts_known"), 1)
            dve.wait_ge(sem("parts_known"), 1)

            def lows_after(n):
                for i in slots_after(n):
                    if i % 2:
                        weight_low(dve, i)

            def crow_copy():
                dve.wait_ge(sem("crow_done"), 1)
                dve.tensor_copy(crow[:], ps[5][0:96, :].bitcast(BF16)[:, 0:T]).then_inc(sem("crow_copied"), 1)

            def conv(n):
                f = FEAT[n]
                dve.wait_ge(sem("up_copied"), n + 1)
                if n >= 2:
                    dve.wait_ge(sem("x_silu"), n - 1)
                tap = [cvec[:, CV_TAP + 12 * t + f:CV_TAP + 12 * t + f + 1] for t in range(CONV_K)]
                a = acc[:, n % 2, :]
                dve.tensor_scalar(a, up[:, n % 2, 3:3 + T], tap[3], cvec[:, CV_CB + f:CV_CB + f + 1], ALU.mult, ALU.add)\
                    .then_inc(sem("dve_seq"), 1)
                dve.wait_ge(sem("dve_seq"), step())
                for t in (2, 1, 0):
                    ins = dve.scalar_tensor_tensor(out=a, in0=up[:, n % 2, t:t + T], scalar=tap[t], in1=a, op0=ALU.mult, op1=ALU.add)
                    if t:
                        ins.then_inc(sem("dve_seq"), 1)
                        dve.wait_ge(sem("dve_seq"), step())
                ins.then_inc(sem("conv_done"), 1)

            def x_rows(q):
                dve.wait_ge(sem("x_transposed"), q + 1)
                f = FEAT[TRANSPOSED[q]]
                dst = X[:, :, f * P:(f + 1) * P] if f < 8 else Btm[:, :, (f - 8) * P:(f - 7) * P]
                dve.tensor_copy(dst, tbank(T_X + q)[:].rearrange("p (c t) -> p c t", c=TC)).then_inc(sem("x_rows"), 1)

            tr = 0
            for n in range(N_QK):
                if n < N_Z:
                    conv(n)
                if n == 3:
                    crow_copy()
                while tr < 10 and TRANSPOSED[tr] <= n - 2:
                    x_rows(tr)
                    tr += 1
                if n == N_Z + 1:
                    dve.wait_ge(sem("decays_exp"), 3)
                    dve.tensor_tensor(dte[:], dte[:], sp[:, :, 0:H], ALU.mult).then_inc(sem("scales_known"), 1)
                    dve.wait_ge(sem("scales_known"), 1)
                lows_after(n)

            def qk_sum(i):
                dve.wait_ge(sem("qk_squared"), i + 1)
                dve.tensor_reduce(qss[:, i, :], heads(m["sq"][:]), AX, ALU.add).then_inc(sem("qk_sum"), 1)

            def qk_scale(i):
                dve.wait_ge(sem("qk_rstd"), i + 1)
                if i >= 2:
                    dve.wait_ge(sem("qk_transposed"), i - 1)
                dve.tensor_tensor(heads(m["qn"][:, i % 2, :]), heads(ps[i % 2][:]), over(qr[:, i, :], P, 8, HD), ALU.mult)\
                    .then_inc(sem("qk_scaled"), 1)

            def m_product(c, w):
                v = 4 * c + w
                dve.wait_ge(sem("decay_exp"), v + 1)
                dve.wait_ge(sem("cb_copied"), c + 1)
                if v >= 2:
                    dve.wait_ge(sem("diag_done"), v - 1)
                g = w // 2
                for h in range(4 * w, 4 * w + 4):
                    q = slice((h % 4) * P, (h % 4 + 1) * P)
                    last = dve.scalar_tensor_tensor(out=M[:, w % 2, q], in0=dec[:, w % 2, q], scalar=sp[:, c, h:h + 1],
                                                    in1=cbs[:, g * P:(g + 1) * P], op0=ALU.mult, op1=ALU.mult)
                last.then_inc(sem("m_done"), 1)

            def y_add(c, g):
                cols = slice(g * BLK, (g + 1) * BLK)
                dve.wait_ge(sem("diag_done"), 4 * c + 2 * g + 2)
                dve.wait_ge(sem("y_skip"), c + 1)
                dve.tensor_tensor(y[:, cols], y[:, cols], ps[7][:], ALU.add).then_inc(sem("y_diag"), 1)
                dve.wait_ge(sem("y_diag"), 2 * c + g + 1)
                if c:
                    dve.wait_ge(sem("y_off_done"), 2 * (c - 1) + g + 1)
                    dve.tensor_tensor(heads(yo[:]), heads(ps[4][:]), over(ecum[:, c, 8 * g:8 * g + 8], P, 8, HD), ALU.mult)\
                        .then_inc(sem("y_off_scaled"), 1)
                    dve.wait_ge(sem("y_off_scaled"), 2 * (c - 1) + g + 1)
                    dve.tensor_tensor(y[:, cols], y[:, cols], yo[:], ALU.add).then_inc(sem("y_whole"), 1)
                else:
                    dve.tensor_copy(y[:, cols], y[:, cols]).then_inc(sem("y_whole"), 1)

            def state_keep(c, g):
                cols = slice(g * BLK, (g + 1) * BLK)
                if c:
                    dve.wait_ge(sem("y_off_done"), 2 * (c - 1) + g + 1)
                    dve.tensor_tensor(heads(Hst[:, cols]), heads(Hst[:, cols]), over(etot[:, c, 8 * g:8 * g + 8], P, 8, HD), ALU.mult)\
                        .then_inc(sem("dve_seq"), 1)
                    dve.wait_ge(sem("dve_seq"), step())
                dve.wait_ge(sem("state_done"), 2 * c + g + 1)
                bank = ps[4 if g == 0 else 7][:]
                if c:
                    dve.tensor_tensor(Hst[:, cols], Hst[:, cols], bank, ALU.add).then_inc(sem("state_kept"), 1)
                else:
                    dve.tensor_copy(Hst[:, cols], bank).then_inc(sem("state_kept"), 1)
                dve.wait_ge(sem("state_kept"), 2 * c + g + 1)

            for i in range(16):
                qk_sum(i)
                qk_scale(i)
                c = i // 4
                if i % 4 == 0:
                    m_product(c, 0)
                    m_product(c, 1)
                if i % 4 == 1:
                    m_product(c, 2)
                    m_product(c, 3)
                    y_add(c, 0)
                if i % 4 == 2:
                    y_add(c, 1)
                if i % 4 == 3 and c < TC - 1:
                    state_keep(c, 0)
                    state_keep(c, 1)
                lows_after(N_QK + i)
            def yT_scale(k, group):
                dve.wait_ge(sem("sy_transposed" if group == 0 else "ay_transposed"), k + 1)
                if k >= 2:
                    low_made(dve, "yT", group * KC + k - 2)
                col = (CV_SSM, CV_ATT)[group] + k
                dve.tensor_scalar(yTf[:, k % 2, :], tbank((T_SY, T_AY)[group] + k)[:], cvec[:, col:col + 1], None, ALU.mult)\
                    .then_inc(sem("yT_scaled"), 1)

            for n in range(N_V, N_SO):
                lows_after(n)
                for k in SSD_OUT.get(n - N_V, ()):
                    yT_scale(k, 0)
                    if k % 2 == 0 and k:
                        output_low(dve, k - 1, 0)
                if n == N_V + 5:
                    output_low(dve, KC - 1, 0)

            def add_residual(i):
                n = N_SO + i
                dve.wait_ge(sem("pass_done"), n + 1)
                r = rs_s if i < 8 else rs_a
                dst = zs[:, i % 4, (i // 4 % 2) * BLK:(i // 4 % 2 + 1) * BLK]
                dve.scalar_tensor_tensor(out=dst, in0=ps[n % 2][:], scalar=r[:, i % 4:i % 4 + 1], in1=dst, op0=ALU.mult, op1=ALU.add)\
                    .then_inc(sem("residual_added"), 1)
                lows_after(n)

            dve.wait_ge(sem("residual_in"), 16)
            dve.wait_ge(sem("y_rstd"), 1)
            for i in range(8):
                add_residual(i)

            def row_max(v):
                n = P * (v // H + 1)
                dve.wait_ge(sem("s_done"), v + 1)
                dve.tensor_reduce(nmax[:, v:v + 1], ps[4 + v % 3][:, 0:n], AX, ALU.max, negate=True).then_inc(sem("max_known"), 1)

            def pt_store(v):
                n = P * (v // H + 1)
                dve.wait_ge(sem("p_transposed"), v + 1)
                if v >= 2:
                    dve.wait_ge(sem("pv_done"), v - 1)
                dve.tensor_copy(PT[:, v % 2, 0:n], tbank(T_P + v)[:, 0:n]).then_inc(sem("pt_stored_dve"), 1)

            def ya_store(w):
                qb, g = divmod(w, 2)
                dve.wait_ge(sem("pv_done"), 8 * w + 8)
                dve.reciprocal(rinv[:, 8 * w:8 * w + 8], rsum[:, 8 * w:8 * w + 8]).then_inc(sem("dve_seq"), 1)
                dve.wait_ge(sem("dve_seq"), step())
                if w == 0:
                    dve.wait_ge(sem("pass_done"), N_AO)
                dve.tensor_tensor(heads(ya[:, qb, g * BLK:(g + 1) * BLK]), heads(ps[w % 2][:]), over(rinv[:, 8 * w:8 * w + 8], P, 8, HD),
                                  ALU.mult).then_inc(sem("ya_stored"), 1)

            for v in range(NU + 4):
                if v < NU:
                    row_max(v)
                if 1 <= v <= NU and (v - 1) % 2 == 1:
                    pt_store(v - 1)
                if v >= 4 and (v - 4) % 8 == 7:
                    ya_store((v - 4) // 8)
            for k in range(KC + 1):
                if k < KC:
                    yT_scale(k, 1)
                if k % 2 == 0 and k:
                    output_low(dve, k - 1, 1)
            dve.wait_ge(sem("ya_rstd"), 1)
            dve.wait_ge(sem("residual_added"), 8)
            for i in range(8, 16):
                add_residual(i)

            dve.wait_ge(sem("f_rstd"), 1)
            dve.wait_ge(sem("wffn_in"), 16)
            dve.wait_ge(sem("residual_added"), 16)
            for c in range(TC):
                dve.scalar_tensor_tensor(out=xn[:, c, :], in0=zs[:, c, :], scalar=rf[:, c:c + 1], in1=m["wffn"][:], op0=ALU.mult,
                                         op1=ALU.mult).then_inc(sem("xn_scaled"), 1)

            for k in range(1, KC, 2):
                dve.wait_ge(sem("xn_transposed"), k + 1)
                dve.tensor_copy(m["xnT"][:, k, :], tbank(T_XN + k)[:]).then_inc(sem("xnT_stored_dve"), 1)
            dve.wait_ge(sem("router_done"), 1)
            dve.tensor_copy(lgT[0:NG + NE, :], ps[4][0:NG + NE, 0:T // 2]).then_inc(sem("logits_copied"), 1)
            dve.wait_ge(sem("router_rows"), 1)
            dve.wait_ge(sem("rbias_in"), 16 * 2)
            for half in range(2):
                dve.tensor_tensor(lg[:, 2 * half:2 * half + 2, :], ps[5 + half][:, 0:2 * 36].rearrange("p (c e) -> p c e", c=2),
                                  rbias[:].unsqueeze(1).broadcast_to([P, 2, 36]), ALU.add).then_inc(sem("dve_seq"), 1)
                last = step()
            dve.wait_ge(sem("dve_seq"), last)

            def first_max(vals, top, at, tmp, n):
                dve.tensor_reduce(top, vals, AX, ALU.max).then_inc(sem("dve_seq"), 1)
                dve.wait_ge(sem("dve_seq"), step())
                dve.tensor_tensor(tmp, vals, over(top, P, TC, n), ALU.is_lt).then_inc(sem("dve_seq"), 1)
                dve.wait_ge(sem("dve_seq"), step())
                dve.scalar_tensor_tensor(out=tmp, in0=tmp, scalar=float(NE), in1=iota[:, 0:n].unsqueeze(1).broadcast_to([P, TC, n]),
                                         op0=ALU.mult, op1=ALU.add).then_inc(sem("dve_seq"), 1)
                dve.wait_ge(sem("dve_seq"), step())
                dve.tensor_reduce(at, tmp, AX, ALU.min).then_inc(sem("dve_seq"), 1)
                dve.wait_ge(sem("dve_seq"), step())

            def one_hot(dst, at, n):
                dve.tensor_tensor(dst, iota[:, 0:n].unsqueeze(1).broadcast_to([P, TC, n]), over(at, P, TC, n), ALU.is_equal)\
                    .then_inc(sem("dve_seq"), 1)
                dve.wait_ge(sem("dve_seq"), step())

            groups = lg[:, :, 0:NG]
            first_max(groups, gm, gi, goh[:], NG)
            dve.tensor_tensor(gex[:], groups, over(gm, P, TC, NG), ALU.subtract).then_inc(sem("group_shifted"), 1)
            dve.wait_ge(sem("group_shifted"), 1)
            one_hot(goh[:], gi, NG)
            dve.tensor_tensor(gsel[:], lg[:, :, NG:].rearrange("p c (g e) -> p c g e", g=NG), over(goh[:], P, TC, NG, NEG), ALU.mult)\
                .then_inc(sem("dve_seq"), 1)
            dve.wait_ge(sem("dve_seq"), step())
            dve.tensor_reduce(sel[:], gsel[:].rearrange("p c g e -> p c e g"), AX, ALU.add).then_inc(sem("dve_seq"), 1)
            dve.wait_ge(sem("dve_seq"), step())
            first_max(sel[:], m1, i1, t8[:], NEG)
            one_hot(oh[:], i1, NEG)
            dve.scalar_tensor_tensor(out=sel2[:], in0=oh[:], scalar=MASKED, in1=sel[:], op0=ALU.mult, op1=ALU.add)\
                .then_inc(sem("dve_seq"), 1)
            dve.wait_ge(sem("dve_seq"), step())
            first_max(sel2[:], m2, i2, t8[:], NEG)
            dve.tensor_tensor(e2, m2, m1, ALU.subtract).then_inc(sem("pair_diff"), 1)
            for k, at in ((0, i1), (1, i2)):
                dve.scalar_tensor_tensor(out=eid[:, k, :], in0=gi, scalar=float(NEG), in1=at, op0=ALU.mult, op1=ALU.add)\
                    .then_inc(sem("dve_seq"), 1)
                last = step()
            dve.wait_ge(sem("dve_seq"), last)
            dve.tensor_tensor(E12[:].rearrange("p k c e -> p (k c) e"), iota[:].unsqueeze(1).broadcast_to([P, 2 * TC, NE]),
                              over(eid[:].rearrange("p k c -> p (k c)"), P, 2 * TC, NE), ALU.is_equal).then_inc(sem("dve_seq"), 1)
            dve.wait_ge(sem("dve_seq"), step())
            dve.tensor_tensor(occ[:], E12[:, 0], E12[:, 1], ALU.add).then_inc(sem("occupied"), 1)
            dve.wait_ge(sem("group_exp"), 1)
            dve.tensor_reduce(zg, gex[:], AX, ALU.add).then_inc(sem("dve_seq"), 1)
            dve.wait_ge(sem("dve_seq"), step())
            dve.reciprocal(pg, zg).then_inc(sem("dve_seq"), 1)
            dve.wait_ge(sem("pair_exp"), 1)
            dve.tensor_scalar(e21, e2, 1.0, None, ALU.add).then_inc(sem("dve_seq"), 1)
            step()
            dve.wait_ge(sem("dve_seq"), step())
            dve.reciprocal(inv, e21).then_inc(sem("dve_seq"), 1)
            dve.wait_ge(sem("dve_seq"), step())
            gates = pay[:, :, :, 2].bitcast(F32)
            dve.wait_ge(sem("tokens_known"), 1)
            dve.tensor_tensor(gates[:, 0, :], inv, pg, ALU.mult).then_inc(sem("dve_seq"), 1)
            dve.wait_ge(sem("dve_seq"), step())
            dve.tensor_tensor(gates[:, 1, :], e2, gates[:, 0, :], ALU.mult).then_inc(sem("dve_seq"), 1)
            dve.wait_ge(sem("dve_seq"), step())
            dve.wait_ge(sem("ranks_done"), 1)
            dve.tensor_tensor(t12[:], E12[:], ps[7][:, 0:P].rearrange("p (c e) -> p c e", c=TC).unsqueeze(1)
                              .broadcast_to([P, 2, TC, NE]), ALU.mult).then_inc(sem("dve_seq"), 1)
            dve.wait_ge(sem("dve_seq"), step())
            dve.tensor_reduce(place[:], t12[:], AX, ALU.add).then_inc(sem("dve_seq"), 1)
            dve.wait_ge(sem("dve_seq"), step())
            dve.scalar_tensor_tensor(out=dest_i[:], in0=place[:], scalar=float(NE), in1=eid[:], op0=ALU.mult, op1=ALU.add)\
                .then_inc(sem("payload_ready"), 1)
            dve.wait_ge(sem("ranks_done"), 2)
            dve.tensor_reduce(most[:], ps[6][:, 0:NE], AX, ALU.max).then_inc(sem("dve_seq"), 1)
            dve.wait_ge(sem("dve_seq"), step())
            dve.wait_ge(sem("payload_ready"), 1)
            dve.tensor_copy(most_i[:], most[:]).then_inc(sem("most_known"), 1)

            def expert(p, r4, first=False):
                j = r4 % 2
                dve.wait_ge(sem("xg_transposed"), p + 1)
                if not first:
                    dve.wait_ge(sem("gate_up_done"), p - 1)
                dve.tensor_copy(m["xgT"][:, j, 4:8, :].rearrange("p k t -> p (k t)"), ps[3][:]).then_inc(sem("xgT_dve"), 1)
                dve.wait_ge(sem("gate_silu"), p + 1)
                if not first or j:
                    dve.wait_ge(sem("hid_transposed"), p)
                dve.tensor_tensor(m["hid"][:], m["sg"][:], ps[j][:, DE:], ALU.mult).then_inc(sem("hid_done"), 1)
                dve.wait_ge(sem("hid_transposed"), p + 1)
                if not first:
                    dve.wait_ge(sem("down_done"), p - 1)
                dve.tensor_copy(m["hidT"][:, j, :], ps[4][:, 0:DE]).then_inc(sem("hidT_stored"), 1)
                dve.wait_ge(sem("down_done"), p + 1)
                if not first:
                    dve.wait_ge(sem(f"rows_out{j}"), (p - j) * 8)
                dve.tensor_scalar(m["yrow"][:, j, BLK:], ps[7][:], slot[:, r4, 2:3].bitcast(F32), None, ALU.mult)\
                    .then_inc(sem("y_scaled_dve"), 1)

            experts(dve, expert)


_INS = ["x", "norm_mix_w", "w_in", "conv_w", "conv_b", "dt_bias", "a_log", "d_skip", "ssm_norm_w", "q_norm_w", "k_norm_w",
        "fox_f_bias", "att_out_norm_w", "w_out", "norm_ffn_w", "w_router_group", "b_router_group", "w_router_expert",
        "b_router_expert", "w_expert_gate", "w_expert_up", "w_expert_down"]


def kernel(**inputs):
    import numpy as _np
    import concourse.bacc as _bacc
    from concourse import mybir as _mybir
    from concourse.bass_utils import run_bass_kernel_spmd as _run

    nc = _bacc.Bacc("TRN2", target_bir_lowering=False, num_devices=1)
    arrays, args = {}, []
    for name in _INS:
        a = _np.ascontiguousarray(inputs[name])
        arrays[f"in_{name}_dram"] = a
        args.append(nc.dram_tensor(f"in_{name}_dram", a.shape, _mybir.dt.from_np(a.dtype), kind="ExternalInput").ap())
    args.append(nc.dram_tensor("out_0_dram", (1, T, D), _mybir.dt.float32, kind="ExternalOutput").ap())
    hybrid_layer(nc, *args)
    r = _run(nc, [arrays], core_ids=[0])
    return r.results[0]["out_0_dram"]
```
